# Optimizing a Trainium2 kernel written in Bass

```python
import math
import jax, jax.numpy as jnp
from jax import lax
import numpy as np

D_MODEL = 2048
BATCH = 1
SEQ = 256
DEPTH = 2

CHUNK = 64
HEAD_DIM = 128
N_MIX_HEADS = D_MODEL // HEAD_DIM
SB_HEADS = N_MIX_HEADS // 4
GDN_HEADS = N_MIX_HEADS // 2
SWA_HEADS = N_MIX_HEADS // 4
SWA_KV_HEADS = SWA_HEADS // 2
SB_BLOCK = 128
GDN_CONV = 4
SWA_WINDOW = 128
ROPE_THETA = 10000.0
D_FF = ((8 * D_MODEL // 3 + 255) // 256) * 256
FFN_CONV = 3
EPS = 1e-6

SB_WIDTH = SB_HEADS * HEAD_DIM
GDN_WIDTH = GDN_HEADS * HEAD_DIM
SWA_WIDTH = SWA_HEADS * HEAD_DIM
SWA_KV_WIDTH = SWA_KV_HEADS * HEAD_DIM
MIX_WIDTH = SB_WIDTH + GDN_WIDTH + SWA_WIDTH

IN_SIZES = [SB_WIDTH, SB_WIDTH, SB_WIDTH, 3 * GDN_WIDTH, GDN_WIDTH, GDN_HEADS, GDN_HEADS,
            SWA_WIDTH, SWA_KV_WIDTH, SWA_KV_WIDTH]
IN_WIDTH = int(sum(IN_SIZES))
IN_SPLIT_POINTS = [int(v) for v in np.cumsum(IN_SIZES)[:-1]]

kernel_name = "hybrid_sb_gdn_swa_convffn"

def rmsnorm(x, w):
    xf = x.astype(jnp.float32)
    y = xf * lax.rsqrt(jnp.mean(xf * xf, axis=-1, keepdims=True) + EPS)
    return (y * w.astype(jnp.float32)).astype(x.dtype)

def causal_dwconv(x, w):
    k, s = w.shape[0], x.shape[1]
    xp = jnp.pad(x, ((0, 0), (k - 1, 0), (0, 0)))
    y = xp[:, k - 1:k - 1 + s] * w[k - 1]
    for i in range(k - 1):
        y = y + xp[:, i:i + s] * w[i]
    return y

def rope(x, pos):
    d = x.shape[-1]
    half = d // 2
    inv_freq = ROPE_THETA ** (-jnp.arange(half, dtype=jnp.float32) / half)
    ang = pos[:, None] * inv_freq[None, :]
    cos, sin = jnp.cos(ang)[:, None, :], jnp.sin(ang)[:, None, :]
    xf = x.astype(jnp.float32)
    x1, x2 = xf[..., :half], xf[..., half:]
    return jnp.concatenate([x1 * cos - x2 * sin, x2 * cos + x1 * sin], axis=-1).astype(x.dtype)

def l2norm(x):
    return x * lax.rsqrt(jnp.sum(x * x, axis=-1, keepdims=True) + EPS)

def stick_breaking_attention(q, k, v):
    s_len, d = q.shape[1], q.shape[-1]
    scale = d ** -0.5
    qh = q.transpose(0, 2, 1, 3).astype(jnp.float32)
    kh = k.transpose(0, 2, 1, 3).astype(jnp.float32)
    vh = v.transpose(0, 2, 1, 3).astype(jnp.float32)
    outs = []
    for i0 in range(0, s_len, SB_BLOCK):
        n_keys = i0 + SB_BLOCK
        z = jnp.einsum('bhtd,bhsd->bhts', qh[:, :, i0:n_keys], kh[:, :, :n_keys]) * scale
        t_idx = i0 + jnp.arange(SB_BLOCK)
        s_idx = jnp.arange(n_keys)
        causal = s_idx[None, :] < t_idx[:, None]
        log_stay = jnp.where(causal, jax.nn.log_sigmoid(-z), 0.0)
        log_remain = lax.cumsum(log_stay, axis=3, reverse=True) - log_stay
        a = jnp.where(causal, jnp.exp(jax.nn.log_sigmoid(z) + log_remain), 0.0)
        outs.append(jnp.einsum('bhts,bhsd->bhtd', a, vh[:, :, :n_keys]))
    o = jnp.concatenate(outs, axis=2)
    return o.transpose(0, 2, 1, 3)

def gated_deltanet(qkv, z, a, beta_logit, conv_w, a_log, dt_bias, norm_w):
    b, s_len, _ = qkv.shape
    h, d, c = GDN_HEADS, HEAD_DIM, CHUNK
    nc = s_len // c
    f32 = jnp.float32
    qkv = jax.nn.silu(causal_dwconv(qkv.astype(f32), conv_w.astype(f32)))
    q, k, v = jnp.split(qkv, 3, axis=-1)
    q = l2norm(q.reshape(b, s_len, h, d)) * (d ** -0.5)
    k = l2norm(k.reshape(b, s_len, h, d))
    v = v.reshape(b, s_len, h, d)
    g = -jnp.exp(a_log.astype(f32)) * jax.nn.softplus(a.astype(f32) + dt_bias.astype(f32))
    beta = jax.nn.sigmoid(beta_logit.astype(f32))

    def to_chunks(t):
        return t.reshape(b, nc, c, h, d).transpose(0, 3, 1, 2, 4)

    q, k, v = to_chunks(q), to_chunks(k), to_chunks(v)
    g = jnp.cumsum(g.reshape(b, nc, c, h).transpose(0, 3, 1, 2), axis=-1)
    beta = beta.reshape(b, nc, c, h).transpose(0, 3, 1, 2)

    tril = jnp.tril(jnp.ones((c, c), dtype=bool))
    eye = jnp.eye(c, dtype=f32)
    strict = tril & (eye == 0)
    gamma = jnp.exp(jnp.where(tril, g[..., :, None] - g[..., None, :], -jnp.inf))
    kk = jnp.einsum('bhncd,bhnmd->bhncm', k, k)
    m = eye + jnp.where(strict, beta[..., :, None] * kk * gamma, 0.0)
    u = lax.linalg.triangular_solve(m, v * beta[..., None], left_side=True, lower=True, unit_diagonal=True)
    wd = lax.linalg.triangular_solve(m, k * (beta * jnp.exp(g))[..., None], left_side=True, lower=True,
                                     unit_diagonal=True)
    qk = jnp.einsum('bhncd,bhnmd->bhncm', q, k) * gamma
    q_dec = q * jnp.exp(g)[..., None]
    g_last = g[..., -1:]
    k_dec = k * jnp.exp(g_last - g)[..., None]
    decay = jnp.exp(g_last[..., 0])

    def step(state, xs):
        u_n, wd_n, qd_n, qk_n, kd_n, dec_n = xs
        v_new = u_n - jnp.einsum('bhck,bhkv->bhcv', wd_n, state)
        o_n = jnp.einsum('bhck,bhkv->bhcv', qd_n, state) + jnp.einsum('bhcm,bhmv->bhcv', qk_n, v_new)
        state = dec_n[..., None, None] * state + jnp.einsum('bhck,bhcv->bhkv', kd_n, v_new)
        return state, o_n

    xs = tuple(jnp.moveaxis(t, 2, 0) for t in (u, wd, q_dec, qk, k_dec, decay))
    _, o = lax.scan(step, jnp.zeros((b, h, d, d), f32), xs)
    o = o.transpose(1, 0, 3, 2, 4).reshape(b, s_len, h, d)
    zg = jax.nn.silu(z.astype(f32).reshape(b, s_len, h, d))
    o = o * lax.rsqrt(jnp.mean(o * o, axis=-1, keepdims=True) + EPS) * norm_w.astype(f32) * zg
    return o.reshape(b, s_len, h * d)

def sliding_window_attention(q, k, v, sinks, pos):
    b, s_len, hq, d = q.shape
    hkv = k.shape[2]
    grp = hq // hkv
    c = CHUNK
    nc = s_len // c
    nw = SWA_WINDOW // CHUNK
    q = rope(q, pos)
    k = rope(k, pos)
    qc = q.reshape(b, nc, c, hkv, grp, d)
    kc = k.reshape(b, nc, c, hkv, d)
    vc = v.reshape(b, nc, c, hkv, d)

    def band(t):
        parts = [jnp.pad(t, ((0, 0), (i, 0), (0, 0), (0, 0), (0, 0)))[:, :nc] for i in range(nw - 1, -1, -1)]
        return jnp.concatenate(parts, axis=2)

    kb, vb = band(kc), band(vc)
    key_chunk = jnp.arange(nc)[:, None] - (nw - 1) + jnp.arange(nw * c)[None, :] // c
    valid = key_chunk >= 0
    scores = jnp.einsum('bnqhgd,bnkhd->bnhgqk', qc, kb).astype(jnp.float32) * (d ** -0.5)
    scores = jnp.where(valid[None, :, None, None, None, :], scores, -jnp.inf)
    sink = sinks.astype(jnp.float32).reshape(hkv, grp)[None, None, :, :, None, None]
    mx = jnp.maximum(jnp.max(scores, axis=-1, keepdims=True), sink)
    p = jnp.exp(scores - mx)
    probs = p / (jnp.sum(p, axis=-1, keepdims=True) + jnp.exp(sink - mx))
    o = jnp.einsum('bnhgqk,bnkhd->bnqhgd', probs.astype(v.dtype), vb)
    return o.reshape(b, s_len, hq * d)

def hybrid_mixer(h, w_in, gdn_conv, gdn_a_log, gdn_dt_bias, gdn_norm, swa_sinks, w_o, pos):
    b, s_len, _ = h.shape
    proj = h @ w_in
    q_a, k_a, v_a, qkv_b, z_b, a_b, beta_b, q_c, k_c, v_c = jnp.split(proj, IN_SPLIT_POINTS, axis=-1)
    o_a = stick_breaking_attention(q_a.reshape(b, s_len, SB_HEADS, HEAD_DIM),
                                   k_a.reshape(b, s_len, SB_HEADS, HEAD_DIM),
                                   v_a.reshape(b, s_len, SB_HEADS, HEAD_DIM)).reshape(b, s_len, SB_WIDTH)
    o_b = gated_deltanet(qkv_b, z_b, a_b, beta_b, gdn_conv, gdn_a_log, gdn_dt_bias, gdn_norm)
    o_c = sliding_window_attention(q_c.reshape(b, s_len, SWA_HEADS, HEAD_DIM),
                                   k_c.reshape(b, s_len, SWA_KV_HEADS, HEAD_DIM),
                                   v_c.reshape(b, s_len, SWA_KV_HEADS, HEAD_DIM), swa_sinks, pos)
    o = jnp.concatenate([o_a.astype(h.dtype), o_b.astype(h.dtype), o_c.astype(h.dtype)], axis=-1)
    return o @ w_o

def conv_glu_ffn(h, w_up, conv_w, conv_b, w_down):
    gate, val = jnp.split(h @ w_up, 2, axis=-1)
    gate = causal_dwconv(gate, conv_w) + conv_b
    return (jax.nn.silu(gate) * val) @ w_down

def setup_inputs(seed: int = 0) -> dict:
    key = jax.random.key(seed)
    ks = jax.random.split(key, 16)

    def normal(k, shape, scale):
        return jax.random.normal(k, shape, jnp.float32) * scale

    dt = jnp.exp(jax.random.uniform(ks[5], (DEPTH, GDN_HEADS), jnp.float32,
                                    minval=math.log(1e-3), maxval=math.log(1e-1)))
    return {
        "x": normal(ks[0], (BATCH, SEQ, D_MODEL), 1.0),
        "attn_norm": 1.0 + normal(ks[1], (DEPTH, D_MODEL), 0.02),
        "w_in": normal(ks[2], (DEPTH, D_MODEL, IN_WIDTH), D_MODEL ** -0.5),
        "gdn_conv": normal(ks[3], (DEPTH, GDN_CONV, 3 * GDN_WIDTH), GDN_CONV ** -0.5),
        "gdn_a_log": jnp.log(jax.random.uniform(ks[4], (DEPTH, GDN_HEADS), jnp.float32, minval=1.0, maxval=16.0)),
        "gdn_dt_bias": dt + jnp.log(-jnp.expm1(-dt)),
        "gdn_norm": 1.0 + normal(ks[6], (DEPTH, HEAD_DIM), 0.02),
        "swa_sinks": normal(ks[7], (DEPTH, SWA_HEADS), 1.0),
        "w_o": normal(ks[8], (DEPTH, MIX_WIDTH, D_MODEL), MIX_WIDTH ** -0.5),
        "ffn_norm": 1.0 + normal(ks[9], (DEPTH, D_MODEL), 0.02),
        "w_up": normal(ks[10], (DEPTH, D_MODEL, 2 * D_FF), D_MODEL ** -0.5),
        "ffn_conv": normal(ks[11], (DEPTH, FFN_CONV, D_FF), FFN_CONV ** -0.5),
        "ffn_conv_bias": normal(ks[12], (DEPTH, D_FF), 0.02),
        "w_down": normal(ks[13], (DEPTH, D_FF, D_MODEL), D_FF ** -0.5),
        "final_norm": 1.0 + normal(ks[14], (D_MODEL,), 0.02),
    }

def reference(x, attn_norm, w_in, gdn_conv, gdn_a_log, gdn_dt_bias, gdn_norm, swa_sinks, w_o,
              ffn_norm, w_up, ffn_conv, ffn_conv_bias, w_down, final_norm):
    pos = jnp.arange(x.shape[1], dtype=jnp.float32)
    for l in range(DEPTH):
        x = x + hybrid_mixer(rmsnorm(x, attn_norm[l]), w_in[l], gdn_conv[l], gdn_a_log[l], gdn_dt_bias[l],
                             gdn_norm[l], swa_sinks[l], w_o[l], pos)
        x = x + conv_glu_ffn(rmsnorm(x, ffn_norm[l]), w_up[l], ffn_conv[l], ffn_conv_bias[l], w_down[l])
    return rmsnorm(x, final_norm)


_drawn_inputs = setup_inputs


def setup_inputs(seed=0):
    import zlib

    import numpy as np

    out = dict(_drawn_inputs(seed))
    spreads = {}
    factors = {'gdn_norm': 4.617,
     'swa_sinks': 64.0,
     'ffn_norm': 2.83,
     'ffn_conv_bias': 4.217,
     'final_norm': 7.764}
    for name, (base, spread) in spreads.items():
        noise = np.random.default_rng([zlib.crc32(name.encode()), seed]).standard_normal(out[name].shape)
        drawn = base * np.exp(spread * noise) if base else spread * noise
        out[name] = __import__('jax').numpy.asarray(drawn.astype(out[name].dtype))
    for name, factor in factors.items():
        out[name] = (out[name] * factor).astype(out[name].dtype)
    return out
```

```python
import concourse.bass as bass
from concourse import mybir

F32 = mybir.dt.float32
F32R = mybir.dt.float32r
ACT = mybir.ActivationFunctionType
ALU = mybir.AluOpType
AX = mybir.AxisListType

P = 128
D = 2048
T = 256
DEPTH = 2
KC = D // P
GH, SH, WH_, KVH = 8, 4, 4, 2
CH = 64
DFF = 5632
FC = DFF // P
F_PARTS = (24, 20)
SCALE = float(P) ** -0.5
EPS = 1e-6
NORMS = 2 * DEPTH + 1
AHEAD = 2
SLOTS = 4

IN_ORDER = ["q0", "k0", "v0", "z0", "q1", "k1", "v1", "sb0", "sb1", "sb2", "z1", "sw0", "sw1"]
IN_TILES = len(IN_ORDER)
U_IN = IN_TILES * 4
U_O = 16
U_UP = [F_PARTS[0] // 4 * 8, F_PARTS[1] // 4 * 8]
U_DN = [F_PARTS[0] // 4 * 4, F_PARTS[1] // 4 * 4]
U_LAYER = U_IN + U_O + sum(U_UP) + sum(U_DN)
U_ALL = DEPTH * U_LAYER
E_IN, E_O = IN_TILES * 4, 32
E_UP = [F_PARTS[0] * 2, F_PARTS[1] * 2]
E_DN = [16, 16]
E_LAYER = E_IN + E_O + sum(E_UP) + sum(E_DN)

PAR_GC, PAR_FCW, PAR_FB, PAR_GN, PAR_SK, PAR_N = 0, 96, 228, 272, 273, 277

CONST = {"rot": 128, "negu": 128, "negone": 128, "sbmask": 384, "sbadd": 384, "cos": 256, "sin": 256,
         "swaadd": 512, "gmask": 128, "level": 768, "reset": 256}
CONST_AT, _at = {}, 0
for _n, _w in CONST.items():
    CONST_AT[_n] = _at
    _at += _w
CONST_N = _at


class Signal:

    def __init__(self, sem, per_layer, before):
        self.sem, self.per_layer, self.before = sem, per_layer, before

    def of(self, l, k):
        return l * self.per_layer + (self.before + k)


GATES_FROM, GDN_FROM, SB_FROM, SW_FROM = 1, 3, 10, 12


def beats(n):
    for _ in range(n):
        yield


class Strands:

    def __init__(self):
        self.running = []

    def begin(self, strand):
        self.running.append(strand)

    def beat(self):
        for strand in self.running:
            next(strand, None)

    def beats(self, n):
        for _ in range(n):
            self.beat()

    def finish(self):
        for strand in self.running:
            for _ in strand:
                pass
        self.running = []


def build(nc, units, wab, params, gate_par, consts, ident_ones, x_in, norm_w, out):
    off = [16512]

    def place(name, cols, dt=F32, at=None):
        if at is None:
            at = off[0]
            off[0] += cols * 4
        return nc.alloc_sbuf_tensor_at(name, [P, cols], dt, offset=at)[:, :]

    def here():
        return off[0]

    XT = place("residual", KC * T).rearrange("p (k t) -> p k t", k=KC)
    XHL = place("x_hi_lo", KC * 2 * T, F32R).rearrange("p (k t) -> p k t", k=KC)
    w_hi = place("w_hi", SLOTS * 2048, F32R).rearrange("p (s k n) -> p s k n", s=SLOTS, k=4)
    raw_at = here()
    w_lo = place("w_lo", SLOTS * 2048, F32R).rearrange("p (s k n) -> p s k n", s=SLOTS, k=4)
    w_raw = place("w_raw", SLOTS * 2048, F32, at=raw_at).rearrange("p (s k n) -> p s k n", s=SLOTS, k=4)
    PAR = place("params", 280)
    NW = place("norm_weights", NORMS * KC)
    GPAR = place("gate_params", 8)
    IO = place("ident_ones", 256)
    IDENT, ONES = IO[:, 0:128], IO[:, 128:256]
    RSTD = place("rstd_rows", T)
    LO = place("lo_ring", 2 * T).rearrange("p (s t) -> p s t", s=2)
    SUM = place("sum_ring", 2 * T).rearrange("p (s t) -> p s t", s=2)
    SMALL = place("small", 128)
    MS2, R2 = SMALL[:, 0:2], SMALL[:, 2:4]
    MHALF = SMALL[:, 4:12]
    SS, RR = SMALL[:, 16:24], SMALL[:, 24:32]
    CO = SMALL[:, 32:48].rearrange("p (c b) -> p c b", c=4)
    MSO, RO = SMALL[:, 48:52], SMALL[:, 52:56]
    MX, NM, SUMP, SE, DEN, REC = (SMALL[:, 56 + 2 * i:58 + 2 * i] for i in range(6))
    EXPA = SMALL[:, 70:71]
    M0 = here()

    def at(name, start, cols, dt=F32):
        assert M0 + (start + cols) * 4 <= 229344, name
        return place(name, cols, dt, at=M0 + start * 4)

    CON = at("consts", 0, CONST_N)
    con = {n: CON[:, CONST_AT[n]:CONST_AT[n] + w] for n, w in CONST.items()}
    m = CONST_N
    QKV = at("gdn_qkv", m, 24 * T).rearrange("p (c t) -> p c t", c=24)
    QKVb = [at(f"gdn_qkv_{i}", m + i * 8 * T, 8 * T) for i in range(3)]
    m += 24 * T
    Z = at("gdn_z", m, 8 * T).rearrange("p (c t) -> p c t", c=8)
    m += 8 * T
    SBX = at("sb_qkv", m, 12 * T).rearrange("p (c t) -> p c t", c=12)
    WABH = at("wab_hi", m, 1024, F32R).rearrange("p (k n) -> p k n", k=KC)
    WABL = at("wab_lo", m + 1024, 1024, F32R).rearrange("p (k n) -> p k n", k=KC)
    WABR = at("wab_raw", m + 1024, 1024).rearrange("p (k n) -> p k n", k=KC)
    m += 12 * T
    SWX = at("swa_qkv", m, 8 * T).rearrange("p (c t) -> p c t", c=8)
    CV = at("conv_in", m, 4 * 260).rearrange("p (s t) -> p s t", s=4)
    CY = at("conv_out", m + 4 * 260, 2 * T).rearrange("p (s t) -> p s t", s=2)
    m += 8 * T
    ST = at("gate_rows", m, T)
    COL = at("gate_cols", m + T, T).rearrange("p (t r) -> p t r", t=2)
    BE = at("beta_eg", m + 2 * T, 16).rearrange("p (t h) -> p t h", t=2)
    DEC = at("chunk_decay", m + 2 * T + 16, 32)
    m += 2 * T + 48
    A0 = m
    A = [at(f"scratch{i}", A0 + 512 * i, 512) for i in range(10)]
    G = [at(f"gate_tmp{i}", A0 + 2048 + T * i, T) for i in range(8)]
    S_ = [None] + [at(f"state{n}", A0 + 6 * 512 + 256 * (n - 1), 256) for n in (1, 2, 3)]
    KF, VF = QKVb[1][:, 0:1024], QKVb[2][:, 0:1024]
    SBZ, SBE, SBV = KF[:, 0:384], KF[:, 384:768], KF[:, 768:1024]
    SBL, SBM = VF[:, 0:384], VF[:, 384:768]
    SWS, SWP = KF[:, 0:512], KF[:, 512:1024]
    SWV, SWT = VF[:, 0:512], VF[:, 512:896]
    MID = at("mid_hi_lo", 0, F_PARTS[0] * 2 * T, F32R).rearrange("p (k t) -> p k t", k=F_PARTS[0])
    f = F_PARTS[0] * 2 * T
    GP = at("gate_in", f, 4 * 260).rearrange("p (s t) -> p s t", s=4)
    GY = at("gate_out", f + 4 * 260, 4 * T).rearrange("p (s t) -> p s t", s=4)
    VV = at("value", f + 4 * 260 + 4 * T, 4 * T).rearrange("p (s t) -> p s t", s=4)
    SQ0 = [at(f"first_squares_{j}", CONST_N + 1024 * j, 1024) for j in range(4)]
    XW0 = [at(f"first_x_times_w_{j}", CONST_N + 4096 + 1024 * j, 1024) for j in range(4)]
    f = A0
    SQ = at("squares", f, 1024)
    PART = at("part_sums", f + 1024, 4 * T).rearrange("p (s t) -> p s t", s=4)
    XW = at("x_times_w", f + 2048, 1024)
    DIAG = at("rstd_diag", f + 3072, T)

    PS = nc.alloc_psum_tensor("banks", [P, 8, 512], F32)

    def signal(name, per_layer=0, before=0):
        return Signal(nc.alloc_semaphore(name), per_layer, before)

    x_loaded = [signal(f"x_loaded_{j}") for j in range(4)]
    io_loaded = signal("io_loaded")
    nw_loaded = signal("nw_loaded")
    par_loaded = signal("par_loaded", 16 * 3)
    con_loaded = signal("con_loaded", 16)
    wab_loaded = signal("wab_loaded", 16)
    whi_ready = signal("whi_ready", 2 * U_LAYER)
    wlo_ready = signal("wlo_ready", 2 * U_LAYER)
    unit_used = signal("unit_used", U_LAYER)
    bank_done = signal("bank_done", E_LAYER // 4 * 3)
    lo_ready = signal("lo_ready", E_LAYER)
    sum_ready = signal("sum_ready", E_LAYER, 4)
    chunk_done = signal("chunk_done", E_LAYER, 2)
    sq_ready = signal("sq_ready", 8)
    part_ready = signal("part_ready", 8)
    xw_ready = signal("xw_ready", 8)
    xhi_ready = signal("xhi_ready", 8)
    xlo_ready = signal("xlo_ready", 8)
    colsum_done = signal("colsum_done", 2)
    ms_ready = signal("ms_ready", 2)
    r_ready = signal("r_ready", 2)
    diag_ready = signal("diag_ready", 2)
    rstd_row_done = signal("rstd_row_done", 2)
    rstd_ready = signal("rstd_ready", 2)
    set_up = signal("set_up")
    pads_ready = signal("pads_ready", 1)
    tap0_ready = signal("tap0_ready", 24)
    tap_done = signal("tap_done", 72)
    silu_done = signal("silu_done", 32)
    gtap0_ready = signal("gtap0_ready", FC)
    gtap_done = signal("gtap_done", 2 * FC)
    gsilu_done = signal("gsilu_done", FC)
    gated_done = signal("gated_done", FC)
    midhi_ready = signal("midhi_ready", FC)
    midlo_ready = signal("midlo_ready", FC)
    wabhi_ready = signal("wabhi_ready", 1)
    wablo_ready = signal("wablo_ready", 1)
    ab_done = signal("ab_done", 1)
    ga = signal("ga", 7)
    gd = signal("gd", 10)
    gate_t_done = signal("gate_t_done", 1)
    dec_done = signal("dec_done", 1)
    gate_cols_ready = signal("gate_cols_ready", 3)
    nat_done = signal("nat_done", 12)
    sqn_ready = signal("sqn_ready", 8)
    ss_ready = signal("ss_ready", 12)
    rr_ready = signal("rr_ready", 4)
    co_ready = signal("co_ready", 16)
    nat_ready = signal("nat_ready", 24)
    back_done = signal("back_done", 12)
    back_ready = signal("back_ready", 12)
    grow_done = signal("grow_done", 4)
    beta_done = signal("beta_done", 4)
    kk_done = signal("kk_done", 4)
    qk_done = signal("qk_done", 4)
    gm_ready = signal("gm_ready", 4)
    e1_ready = signal("e1_ready", 4)
    qkg_ready = signal("qkg_ready", 4)
    w1_ready = signal("w1_ready", 4)
    at_ready = signal("at_ready", 4)
    bt_ready = signal("bt_ready", 24)
    e0_ready = signal("e0_ready", 4)
    x_done = signal("x_done", 24)
    xs_ready = signal("xs_ready", 20)
    dx_done = signal("dx_done", 16)
    ex_done = signal("ex_done", 20)
    d_ready = signal("d_ready", 20)
    e_ready = signal("e_ready", 20)
    u_done = signal("u_done", 4)
    wdt_done = signal("wdt_done", 4)
    wd_done = signal("wd_done", 4)
    u_ready = signal("u_ready", 4)
    wdt_ready = signal("wdt_ready", 4)
    wd_ready = signal("wd_ready", 4)
    kv_done = signal("kv_done", 4)
    mt_done = signal("mt_done", 4)
    mt_ready = signal("mt_ready", 4)
    mst_done = signal("mst_done", 8)
    ds_ready = signal("ds_ready", 8)
    s_ready = signal("s_ready", 12)
    ws_done = signal("ws_done", 4)
    v_ready = signal("v_ready", 4)
    o_done = signal("o_done", 4)
    os_ready = signal("os_ready", 4)
    osq_ready = signal("osq_ready", 4)
    osum_done = signal("osum_done", 4)
    mso_ready = signal("mso_ready", 4)
    ro_ready = signal("ro_ready", 4)
    odiag_ready = signal("odiag_ready", 4)
    orow_done = signal("orow_done", 4)
    oz_ready = signal("oz_ready", 4)
    gdn_out = signal("gdn_out", 4)
    sb_z_done = signal("sb_z_done", 4)
    sb_vt_done = signal("sb_vt_done", 4)
    sb_zs = signal("sb_zs", 4)
    sb_abs = signal("sb_abs", 4)
    sb_exp = signal("sb_exp", 4)
    sb_ln = signal("sb_ln", 4)
    sb_v = signal("sb_v", 8)
    sb_zm = signal("sb_zm", 4)
    sb_sp = signal("sb_sp", 8)
    sb_c_done = signal("sb_c_done", 4)
    sb_y = signal("sb_y", 4)
    sb_a = signal("sb_a", 4)
    sb_o_done = signal("sb_o_done", 4)
    sb_out = signal("sb_out", 4)
    rot_done = signal("rot_done", 3)
    xcos = signal("xcos", 3)
    xsin = signal("xsin", 3)
    roped = signal("roped", 3)
    sw_vt_done = signal("sw_vt_done", 1)
    sw_v = signal("sw_v", 1)
    sw_s_done = signal("sw_s_done", 4)
    sw_s = signal("sw_s", 12)
    sw_p = signal("sw_p", 12)
    sw_den = signal("sw_den", 12)
    sw_pt_done = signal("sw_pt_done", 4)
    sw_pt = signal("sw_pt", 4)
    sw_o_done = signal("sw_o_done", 4)
    sw_out = signal("sw_out", 4)
    ohi_ready = signal("ohi_ready", 4)
    olo_ready = signal("olo_ready", 4)
    stored = signal("stored")
    fin_y = signal("fin_y")
    fin_xw = signal("fin_xw")
    last_xw = signal("last_xw")

    raw_ready = [nc.alloc_semaphore(f"raw_ready_{s}") for s in range(SLOTS)]


    u_o, e_o = U_IN, E_IN
    u_up = [u_o + U_O, u_o + U_O + U_UP[0] + U_DN[0]]
    u_dn = [u_up[0] + U_UP[0], u_up[1] + U_UP[1]]
    e_up = [e_o + E_O, e_o + E_O + E_UP[0] + E_DN[0]]
    e_dn = [e_up[0] + E_UP[0], e_up[1] + E_UP[1]]

    def conv_group(name):
        return {"q": 0, "k": 8, "v": 16}[name[0]] + 4 * int(name[1]) if name[0] in "qkv" else None

    n_conv = lambda i: sum(IN_ORDER[j][0] in "qkv" for j in range(i))
    n_silu = lambda i: sum(IN_ORDER[j][0] in "qkvz" for j in range(i))

    def blk(t, i):
        return slice((2 * t + i) * P, (2 * t + i + 1) * P)

    def b4(ap):
        return ap.rearrange("p (b c) -> p b c", b=4)

    def pair(ap3, c0):
        return ap3[:, c0:c0 + 2, :].rearrange("p i (t c) -> p t i c", t=2)

    def tb(ap, n=P):
        return ap.unsqueeze(2).to_broadcast([P, 4, n])

    def b22(ap):
        return ap.rearrange("p (t i c) -> p t i c", t=2, i=2)

    def KNT(g):
        return QKVb[1][:, 512 * g:512 * g + 512]

    def QNT(g):
        return QKVb[0][:, 512 * g:512 * g + 512]

    def QET(g):
        return QKVb[2][:, 512 * g:512 * g + 512]

    block = nc.Block()
    block.__enter__()

    @block.sync
    def _(sp):
        sp.dma_start(NW, norm_w).then_inc(nw_loaded.sem, 16)

        def load(u, s):
            sp.dma_start(w_raw[:, s].rearrange("p k n -> p (k n)"),
                         units[bass.ds(u, 1)].rearrange("a p n -> p (a n)")).then_inc(raw_ready[s], 16)

        for s in range(SLOTS):
            sp.dma_start(XT[:, 4 * s:4 * s + 4, :], x_in[:, 4 * s:4 * s + 4, :]).then_inc(x_loaded[s].sem, 16)
            if s == 1:
                sp.dma_start(IO, ident_ones).then_inc(io_loaded.sem, 16)
            if s < AHEAD:
                load(s, s)
        for s in range(AHEAD, SLOTS):
            load(s, s)
        with sp.Fori(1, (U_ALL + SLOTS) // SLOTS) as i:
            for s in range(SLOTS):
                sp.wait_ge(unit_used.sem, i * SLOTS + (s - SLOTS + 1))
                load(i * SLOTS + s, s)
        for j in range(4):
            sp.wait_ge(fin_y.sem, j + 1)
            sp.dma_start(out[:, 4 * j:4 * j + 4, :], XT[:, 4 * j:4 * j + 4, :]).then_inc(stored.sem, 16)
        sp.wait_ge(stored.sem, 64)

    @block.tensor
    def _(pe):
        mm, tr = nc.tensor.matmul, nc.tensor.transpose

        def colsum(done):
            for t in range(2):
                for j in range(4):
                    r = mm(PS[:, 4, t:t + 1], PART[:, j, t * P:(t + 1) * P], ONES[:, 0:1],
                           start=(j == 0), stop=(j == 3))
            r.then_inc(done, 1)

        def rows(done):
            mm(PS[:, 5, 0:T], ONES, DIAG, start=True, stop=True).then_inc(done, 1)

        def layer(l):

            def gemm(u, e, n_units, slot0, rhs, ready=None, after=None, weave=None):
                for j in range(n_units):
                    pe.wait_ge(wlo_ready.sem, wlo_ready.of(l, (u + (j + 1)) * 2))
                    if ready:
                        ready(j)
                    s = (slot0 + j) % SLOTS
                    for n in range(4):
                        if j == 0:
                            pe.wait_ge(sum_ready.sem, sum_ready.of(l, e + (n + 1 - 4)))
                        cols = slice(n * P, (n + 1) * P)
                        for k in range(4):
                            x = rhs(4 * j + k)
                            last = j == n_units - 1 and k == 3
                            mm(PS[:, n, :], w_hi[:, s, k, cols], x, start=(j == 0 and k == 0), stop=False)
                            r = mm(PS[:, n, T:2 * T], w_lo[:, s, k, cols], x[:, 0:T], start=False, stop=last)
                            if k == 3 and n == 3:
                                r.then_inc(unit_used.sem, 1)
                            elif last:
                                r.then_inc(bank_done.sem, 1)
                        if weave:
                            weave()
                    if after:
                        after(j)

            def gates_strand():
                pe.wait_ge(wablo_ready.sem, wablo_ready.of(l, 1))
                for k in range(KC):
                    mm(PS[0:64, 4, :], WABH[:, k, :], XHL[:, k, :], start=(k == 0), stop=False)
                    r = mm(PS[0:64, 4, T:2 * T], WABL[:, k, :], XHL[:, k, 0:T], start=False, stop=(k == KC - 1))
                r.then_inc(ab_done.sem, 1)
                yield from beats(12)
                pe.wait_ge(gd.sem, gd.of(l, 10))
                pe.wait_ge(ga.sem, ga.of(l, 7))
                for t in range(2):
                    r = tr(PS[:, 6, t * P:(t + 1) * P], ST[:, t * P:(t + 1) * P], IDENT)
                r.then_inc(gate_t_done.sem, 1)
                for h in range(GH):
                    r = mm(PS[:, 7, 4 * h:4 * h + 4], IDENT[64:72, 64 + h:65 + h].to_broadcast([8, P]),
                           ST[64:72, CH - 1:T:CH], start=True, stop=True)
                r.then_inc(dec_done.sem, 1)
                yield

            def gdn_strand():
                yield from beats(10)
                pe.wait_ge(gate_cols_ready.sem, gate_cols_ready.of(l, 3))
                for g in range(4):
                    yield from gdn(g)

            def gdn(g):
                hh = 2 * g
                pe.wait_ge(silu_done.sem, silu_done.of(l, 4 * n_silu(3 if g < 2 else 7)))
                if g:
                    pe.wait_ge(gdn_out.sem, gdn_out.of(l, g))
                for b, c in ((4, 8), (5, 0), (6, 16)):
                    for t in range(2):
                        for i in range(2):
                            r = tr(PS[:, b, blk(t, i)], QKV[:, c + hh + i, t * P:(t + 1) * P], IDENT)
                    r.then_inc(nat_done.sem, 1)
                yield from beats(8)
                for b, a, n in ((4, 3, 4), (5, 4, 6), (6, 5, 6)):
                    pe.wait_ge(nat_ready.sem, nat_ready.of(l, 6 * g + n))
                    for q in range(4):
                        r = tr(PS[:, b, q * P:(q + 1) * P], A[a][:, q * P:(q + 1) * P], IDENT)
                    r.then_inc(back_done.sem, 1)
                yield from beats(2)
                pe.wait_ge(back_ready.sem, back_ready.of(l, 3 * g + 3))
                for i in range(2):
                    r = mm(b22(PS[:, 6, :])[:, :, i, :], IDENT[0:8, hh + i:hh + i + 1].to_broadcast([8, P]),
                           ST[0:8, :].rearrange("p (t c) -> p t c", t=2), start=True, stop=True)
                r.then_inc(grow_done.sem, 1)
                for q in range(4):
                    c = slice(q * P, (q + 1) * P)
                    r = mm(PS[:, 4, c], KNT(g)[:, c], KNT(g)[:, c], start=True, stop=True)
                r.then_inc(kk_done.sem, 1)
                for q in range(4):
                    c = slice(q * P, (q + 1) * P)
                    r = mm(PS[:, 5, c], KNT(g)[:, c], QNT(g)[:, c], start=True, stop=True)
                r.then_inc(qk_done.sem, 1)
                yield from beats(2)
                pe.wait_ge(gm_ready.sem, gm_ready.of(l, g + 1))
                for i in range(2):
                    r = mm(b22(PS[:, 6, :])[:, :, i, :],
                           IDENT[32:40, 32 + hh + i:33 + hh + i].to_broadcast([8, P]),
                           ST[32:40, :].rearrange("p (t c) -> p t c", t=2), start=True, stop=True)
                r.then_inc(beta_done.sem, 1)
                yield from beats(5)
                pe.wait_ge(bt_ready.sem, bt_ready.of(l, 6 * g + 1))
                for q in range(4):
                    c = slice(q * P, (q + 1) * P)
                    r = tr(PS[:, 4, c], A[8][:, c], IDENT)
                r.then_inc(x_done.sem, 1)
                yield
                for j in range(1, 6):
                    bt = A[8] if j % 2 == 0 else A[6]
                    pe.wait_ge(bt_ready.sem, bt_ready.of(l, 6 * g + j + 1))
                    pe.wait_ge(d_ready.sem, d_ready.of(l, 5 * g + j))
                    for q in range(4):
                        c = slice(q * P, (q + 1) * P)
                        r = mm(PS[:, 5, c], bt[:, c], A[4][:, c], start=True, stop=True)
                    r.then_inc(x_done.sem, 1)
                    yield
                    pe.wait_ge(xs_ready.sem, xs_ready.of(l, 5 * g + j))
                    if j > 1:
                        pe.wait_ge(e_ready.sem, e_ready.of(l, 5 * g + j - 1))
                    else:
                        pe.wait_ge(e0_ready.sem, e0_ready.of(l, g + 1))
                    if j < 5:
                        for q in range(4):
                            c = slice(q * P, (q + 1) * P)
                            r = mm(PS[:, 4, c], A[5][:, c], A[7][:, c], start=True, stop=True)
                        r.then_inc(dx_done.sem, 1)
                    for q in range(4):
                        c = slice(q * P, (q + 1) * P)
                        r = mm(PS[:, 6, c], A[7][:, c], A[5][:, c], start=True, stop=True)
                    r.then_inc(ex_done.sem, 1)
                    yield
                pe.wait_ge(e_ready.sem, e_ready.of(l, 5 * g + 5))
                for q in range(4):
                    c = slice(q * P, (q + 1) * P)
                    r = mm(PS[:, 4, c], A[5][:, c], A[2][:, c], start=True, stop=True)
                r.then_inc(u_done.sem, 1)
                for q in range(4):
                    c = slice(q * P, (q + 1) * P)
                    r = mm(PS[:, 5, c], A[0][:, c], A[5][:, c], start=True, stop=True)
                r.then_inc(wdt_done.sem, 1)
                for q in range(4):
                    c = slice(q * P, (q + 1) * P)
                    r = mm(PS[:, 6, c], A[5][:, c], A[0][:, c], start=True, stop=True)
                r.then_inc(wd_done.sem, 1)
                yield from beats(3)
                pe.wait_ge(u_ready.sem, u_ready.of(l, g + 1))
                pe.wait_ge(wdt_ready.sem, wdt_ready.of(l, g + 1))
                for n, bank, half in ((0, 4, 0), (2, 4, 1), (1, 5, 0)):
                    t, r0 = n // 2, CH * (n % 2)
                    for i in range(2):
                        r = mm(PS[:, bank, blk(half, i)], A[1][r0:r0 + CH, blk(t, i)], A[2][r0:r0 + CH, blk(t, i)],
                               start=True, stop=True)
                r.then_inc(kv_done.sem, 1)
                pe.wait_ge(wd_ready.sem, wd_ready.of(l, g + 1))
                for n, bank, half in ((1, 5, 1), (2, 6, 0)):
                    t, r0 = n // 2, CH * (n % 2)
                    for i in range(2):
                        r = mm(PS[:, bank, blk(half, i)], A[4][r0:r0 + CH, blk(t, i)], A[1][r0:r0 + CH, blk(t, i)],
                               start=True, stop=True)
                r.then_inc(mt_done.sem, 1)
                yield from beats(3)
                pe.wait_ge(mt_ready.sem, mt_ready.of(l, g + 1))
                for n in (1, 2):
                    pe.wait_ge(s_ready.sem, s_ready.of(l, 3 * g + n))
                    for i in range(2):
                        r = mm(PS[:, 6, i * P:(i + 1) * P], A[8][:, blk(n - 1, i)], S_[n][:, i * P:(i + 1) * P],
                               start=True, stop=True)
                    r.then_inc(mst_done.sem, 1)
                    yield from beats(2)
                pe.wait_ge(s_ready.sem, s_ready.of(l, 3 * g + 3))
                for n in (1, 2, 3):
                    t, r0 = n // 2, CH * (n % 2)
                    for i in range(2):
                        c = slice(blk(t, i).start + r0, blk(t, i).start + r0 + CH)
                        r = mm(PS[r0:r0 + CH, 4, blk(t, i)], A[3][:, c], S_[n][:, i * P:(i + 1) * P],
                               start=True, stop=True)
                r.then_inc(ws_done.sem, 1)
                yield from beats(2)
                pe.wait_ge(v_ready.sem, v_ready.of(l, g + 1))
                for t in range(2):
                    for i in range(2):
                        mm(PS[:, 5, blk(t, i)], A[2][:, blk(t, i)], A[9][:, blk(t, i)], start=True, stop=False)
                        for half in range(2):
                            n = 2 * t + half
                            if n:
                                c = slice(blk(t, i).start + CH * half, blk(t, i).start + CH * (half + 1))
                                r = mm(PS[:, 5, c], S_[n][:, i * P:(i + 1) * P], QET(g)[:, c],
                                       start=False, stop=(half == 1))
                r.then_inc(o_done.sem, 1)
                yield
                pe.wait_ge(osq_ready.sem, osq_ready.of(l, g + 1))
                for q in range(4):
                    r = mm(PS[:, 6, q:q + 1], A[3][:, q * P:(q + 1) * P], ONES[:, 0:1], start=True, stop=True)
                r.then_inc(osum_done.sem, 1)
                yield from beats(2)
                pe.wait_ge(odiag_ready.sem, odiag_ready.of(l, g + 1))
                mm(PS[:, 4, :], ONES, A[4], start=True, stop=True).then_inc(orow_done.sem, 1)
                yield from beats(1)

            def sb_strand():
                yield from beats(4)
                pe.wait_ge(chunk_done.sem, chunk_done.of(l, 40))
                pe.wait_ge(gdn_out.sem, gdn_out.of(l, 2))
                for h in range(SH):
                    q, k, v = SBX[:, h, :], SBX[:, 4 + h, :], SBX[:, 8 + h, :]
                    if h:
                        pe.wait_ge(sb_out.sem, sb_out.of(l, h))
                    mm(PS[:, 7, 0:256], k[:, 0:P], q, start=True, stop=True)
                    mm(PS[:, 7, 256:384], k[:, P:T], q[:, P:T], start=True, stop=True)
                    tr(PS[:, 7, 384:512], v[:, 0:P], IDENT).then_inc(sb_z_done.sem, 1)
                    yield from beats(3)
                    pe.wait_ge(sb_sp.sem, sb_sp.of(l, 2 * h + 2))
                    pe.wait_ge(sb_v.sem, sb_v.of(l, 2 * h + 1))
                    mm(PS[:, 7, 0:256], con["negu"], SBL[:, 0:256], start=True, stop=False)
                    mm(PS[:, 7, 128:256], con["negone"], SBL[:, 256:384], start=False, stop=True)
                    mm(PS[:, 7, 256:384], con["negu"], SBL[:, 256:384], start=True, stop=True)
                    tr(PS[:, 7, 384:512], v[:, P:T], IDENT).then_inc(sb_c_done.sem, 1)
                    yield from beats(2)
                    pe.wait_ge(sb_a.sem, sb_a.of(l, h + 1))
                    pe.wait_ge(sb_v.sem, sb_v.of(l, 2 * h + 2))
                    mm(PS[:, 7, 0:256], SBV[:, 0:P], SBE[:, 0:256], start=True, stop=False)
                    mm(PS[:, 7, 128:256], SBV[:, P:T], SBE[:, 256:384], start=False, stop=True).then_inc(
                        sb_o_done.sem, 1)
                    yield

            def sw_strand():
                yield from beats(8)
                pe.wait_ge(sb_out.sem, sb_out.of(l, 4))
                for c in range(3):
                    pe.wait_ge(chunk_done.sem, chunk_done.of(l, 48 if c < 2 else 52))
                    if c:
                        pe.wait_ge(xsin.sem, xsin.of(l, c))
                    mm(PS[:, 7, :], con["rot"], SWX[:, 2 * c:2 * c + 2, :].rearrange("p a t -> p (a t)"),
                       start=True, stop=True).then_inc(rot_done.sem, 1)
                    yield from beats((3, 6, 1)[c])
                pe.wait_ge(xsin.sem, xsin.of(l, 3))
                for v in range(2):
                    for t in range(2):
                        r = tr(PS[:, 7, blk(v, t)], SWX[:, 6 + v, t * P:(t + 1) * P], IDENT)
                r.then_inc(sw_vt_done.sem, 1)
                yield
                pe.wait_ge(roped.sem, roped.of(l, 3))
                pe.wait_ge(sw_v.sem, sw_v.of(l, 1))
                for h in range(WH_):
                    v = h // (WH_ // KVH)
                    if h:
                        pe.wait_ge(sw_out.sem, sw_out.of(l, h))
                    for t in range(2):
                        r = mm(PS[:, 7, t * T:(t + 1) * T], SWX[:, h, t * P:(t + 1) * P], SWX[:, 4 + v, :],
                               start=True, stop=True)
                    r.then_inc(sw_s_done.sem, 1)
                    yield from beats(5)
                    pe.wait_ge(sw_den.sem, sw_den.of(l, 3 * h + 3))
                    tr(PS[:, 7, 0:P], SWP[:, 0:P], IDENT)
                    tr(PS[:, 7, P:2 * P], SWP[:, T:T + P], IDENT)
                    tr(PS[:, 7, 2 * P:3 * P], SWP[:, T + P:2 * T], IDENT).then_inc(sw_pt_done.sem, 1)
                    yield
                    pe.wait_ge(sw_pt.sem, sw_pt.of(l, h + 1))
                    mm(PS[:, 7, 0:T], SWV[:, blk(v, 0)], SWT[:, 0:T], start=True, stop=False)
                    mm(PS[:, 7, P:T], SWV[:, blk(v, 1)], SWT[:, T:T + P], start=False, stop=True).then_inc(
                        sw_o_done.sem, 1)
                    yield

            def norm(n, j):
                if j == 1:
                    pe.wait_ge(part_ready.sem, part_ready.of(l, 4 * n + 4))
                    colsum(colsum_done.sem)
                elif j == 2:
                    pe.wait_ge(diag_ready.sem, diag_ready.of(l, n + 1))
                    rows(rstd_row_done.sem)

            x_rows = lambda k: XHL[:, k, :]
            strands = Strands()
            for i in range(IN_TILES):
                if i == GATES_FROM:
                    strands.begin(gates_strand())
                if i == GDN_FROM:
                    strands.begin(gdn_strand())
                if i == SB_FROM:
                    strands.begin(sb_strand())
                if i == SW_FROM:
                    strands.begin(sw_strand())
                gemm(4 * i, 4 * i, 4, 0, x_rows, ready=(lambda j: pe.wait_ge(xlo_ready.sem, xlo_ready.of(l, j + 1))) if i == 0 else None,
                     after=(lambda j: norm(0, j)) if i == 0 else None, weave=strands.beat)
            for half in range(2):
                for i in range(4):
                    n = 4 * half + i
                    gemm(u_o + 2 * n, e_o + 4 * n, 2, 2 * n, lambda k, half=half: XHL[:, 8 * half + k, :],
                         ready=lambda j, half=half: pe.wait_ge(olo_ready.sem, olo_ready.of(l, 2 * half + j + 1)), weave=strands.beat)
                strands.finish()
            for part in range(2):
                if part == 0:
                    gemm(u_up[0], e_up[0], 4, 0, x_rows, ready=lambda j: pe.wait_ge(xlo_ready.sem, xlo_ready.of(l, 4 + j + 1)),
                         after=lambda j: norm(1, j))
                    gemm(u_up[0] + 4, e_up[0] + 4, 4, 0, x_rows)
                with pe.Fori(1 - part, F_PARTS[part] // 4) as i:
                    for j in range(2):
                        gemm(i * 8 + (u_up[part] + 4 * j), i * 8 + (e_up[part] + 4 * j), 4, 0, x_rows)
                n_units = F_PARTS[part] // 4
                f0 = sum(F_PARTS[:part])
                mid = lambda k: MID[:, k, :]

                def mid_ready(j, f0=f0):
                    pe.wait_ge(midlo_ready.sem, midlo_ready.of(l, f0 + 4 * j + 4))
                if part == 0:
                    with pe.Fori(0, 2) as i:
                        for j in range(2):
                            gemm(i * (2 * n_units) + (u_dn[0] + j * n_units), i * 8 + (e_dn[0] + 4 * j), n_units,
                                 j * n_units, mid, ready=mid_ready)
                else:
                    for j in range(4):
                        gemm(u_dn[1] + j * n_units, e_dn[1] + 4 * j, n_units, j * n_units, mid, ready=mid_ready)

        pe.wait_ge(io_loaded.sem, 16)
        with pe.Fori(0, DEPTH) as l:
            layer(l)
        pe.wait_ge(part_ready.sem, part_ready.of(DEPTH, 4))
        colsum(colsum_done.sem)
        pe.wait_ge(diag_ready.sem, diag_ready.of(DEPTH, 1))
        rows(rstd_row_done.sem)

    @block.scalar
    def _(act):
        A_ = nc.scalar.activation

        def first_hi(j):
            act.wait_ge(xw_ready.sem, xw_ready.of(0, j + 1))
            A_(XHL[:, 4 * j:4 * j + 4, 0:T], XW0[j].rearrange("p (k t) -> p k t", k=4), ACT.Copy).then_inc(
                xhi_ready.sem, 1)

        def first_squares(j):
            act.wait_ge(x_loaded[j].sem, 16)
            A_(SQ0[j], XT[:, 4 * j:4 * j + 4, :].rearrange("p k t -> p (k t)"), ACT.Square).then_inc(
                sq_ready.sem, 1)

        def norm_tile(l, n, j):
            x4 = XT[:, 4 * j:4 * j + 4, :].rearrange("p k t -> p (k t)")
            if n == 1:
                act.wait_ge(chunk_done.sem, chunk_done.of(l, E_IN + 16 + 4 * j + 4))
            else:
                act.wait_ge(chunk_done.sem, chunk_done.of(l, E_LAYER - 16 + 4 * j + 4))
            act.wait_ge(part_ready.sem, part_ready.of(l, 4 * n + j))
            A_(SQ, x4, ACT.Square).then_inc(sq_ready.sem, 1)
            act.wait_ge(xw_ready.sem, xw_ready.of(l, 4 * n + j + 1))
            if n == 1:
                act.wait_ge(unit_used.sem, unit_used.of(l, U_IN + (7, 8, 15, 16)[j]))
            elif n == 2 and j == 0:
                act.wait_ge(unit_used.sem, unit_used.of(l, u_dn[1]))
            A_(XHL[:, 4 * j:4 * j + 4, 0:T], XW.rearrange("p (k t) -> p k t", k=4), ACT.Copy).then_inc(
                xhi_ready.sem, 1)

        def rstd(l, n):
            act.wait_ge(rstd_row_done.sem, rstd_row_done.of(l, n + 1))
            A_(RSTD, PS[:, 5, 0:T], ACT.Copy).then_inc(rstd_ready.sem, 1)

        def split(turn, s, h=0):
            act.wait_ge(raw_ready[s], turn * 16 + 16)
            A_(w_hi[:, s, 2 * h:2 * h + 2].rearrange("p k n -> p (k n)"),
               w_raw[:, s, 2 * h:2 * h + 2].rearrange("p k n -> p (k n)"), ACT.Copy).then_inc(whi_ready.sem, 1)

        def split_all(turn, s):
            act.wait_ge(raw_ready[s], turn * 16 + 16)
            A_(w_hi[:, s].rearrange("p k n -> p (k n)"), w_raw[:, s].rearrange("p k n -> p (k n)"),
               ACT.Copy).then_inc(whi_ready.sem, 2)

        act.wait_ge(set_up.sem, 1)
        for j in range(AHEAD):
            first_hi(j)
            split_all(0, j)
        first_hi(2)
        first_squares(0)
        first_squares(1)
        first_hi(3)
        first_squares(2)
        first_squares(3)

        def layer(l):

            def splits(u, n, i=0, step=0):
                for j in range(n):
                    v = u + AHEAD + j
                    split_all(l * (U_LAYER // SLOTS) + (i * (step // SLOTS) + v // SLOTS), v % SLOTS)

            def woven_splits(u, n, before=None):
                for j in range(n):
                    if before:
                        before(j)
                    v = u + AHEAD + j
                    for h in range(2):
                        split(l * (U_LAYER // SLOTS) + v // SLOTS, v % SLOTS, h)
                        if j < n - 1:
                            strands.beats(2)

            def lo(e, e4, n, u_last):
                if n < 3:
                    act.wait_ge(bank_done.sem, bank_done.of(l, e4 + (n + 1)))
                else:
                    act.wait_ge(unit_used.sem, unit_used.of(l, u_last))
                act.wait_ge(sum_ready.sem, sum_ready.of(l, e + (n + 1 - 2)))
                A_(LO[:, n % 2, :], PS[:, n, T:2 * T], ACT.Copy).then_inc(lo_ready.sem, 1)

            def tile_lo(u, e, e4, n_units, between=None):
                for n in range(4):
                    lo(e, e4, n, u + n_units)
                    strands.beat()
                    if between:
                        between(n)

            def wab_hi():
                act.wait_ge(wab_loaded.sem, wab_loaded.of(l, 16))
                A_(WABH, WABR, ACT.Copy).then_inc(wabhi_ready.sem, 1)

            def in_tile(i):
                def before(j):
                    if i == 0 and j == 3:
                        rstd(l, 0)
                        wab_hi()
                    elif i == IN_TILES - 1 and j >= 2:
                        o_hi(j - 2)
                woven_splits(4 * i, 4, before)
                if i == 0:
                    act.wait_ge(par_loaded.sem, par_loaded.of(l, 48))
                e, group, z = 4 * i, conv_group(IN_ORDER[i]), IN_ORDER[i][0] == "z"
                c0, s0 = 4 * n_conv(i), 4 * n_silu(i)

                def tap0(n):
                    act.wait_ge(chunk_done.sem, chunk_done.of(l, e + n + 1))
                    if n >= 2:
                        act.wait_ge(silu_done.sem, silu_done.of(l, s0 + n - 1))
                    A_(CY[:, n % 2, :], CV[:, n, 3:3 + T], ACT.Copy,
                       scale=PAR[:, PAR_GC + 3 * 24 + group + n:PAR_GC + 3 * 24 + group + n + 1]).then_inc(
                           tap0_ready.sem, 1)

                def silu(n):
                    act.wait_ge(tap_done.sem, tap_done.of(l, 3 * (c0 + n) + 3))
                    A_(QKV[:, group + n, :], CY[:, n % 2, :], ACT.Silu).then_inc(silu_done.sem, 1)

                def silu_z(n):
                    act.wait_ge(chunk_done.sem, chunk_done.of(l, e + n + 1))
                    zc = Z[:, 4 * int(IN_ORDER[i][1]) + n, :]
                    A_(zc, zc, ACT.Silu).then_inc(silu_done.sem, 1)

                def conv_strand():
                    tap0(0)
                    tap0(1)
                    yield from beats(2)
                    silu(0)
                    tap0(2)
                    yield from beats(2)
                    silu(1)
                    tap0(3)
                    yield from beats(2)
                    silu(2)
                    yield from beats(2)
                    silu(3)

                tile_lo(4 * i, e, 3 * i, 4, (lambda n: silu_z(n - 1) if n else None) if z else None)
                if group is not None:
                    strands.begin(conv_strand())
                elif z:
                    silu_z(3)

            def gates_strand():
                yield
                act.wait_ge(ab_done.sem, ab_done.of(l, 1))
                A_(G[0][0:64, :], PS[0:64, 4, T:2 * T], ACT.Copy).then_inc(ga.sem, 1)
                yield from beats(2)
                act.wait_ge(gd.sem, gd.of(l, 3))
                A_(G[3][0:8, :], G[2][0:8, :], ACT.Abs, bias=GPAR[0:8, 1:2]).then_inc(ga.sem, 1)
                A_(G[4][32:40, :], G[2][32:40, :], ACT.Exp, scale=-1.0).then_inc(ga.sem, 1)
                act.wait_ge(ga.sem, ga.of(l, 2))
                A_(G[3][0:8, :], G[3][0:8, :], ACT.Exp, scale=-1.0).then_inc(ga.sem, 1)
                A_(EXPA[0:8, :], GPAR[0:8, 0:1], ACT.Exp)
                act.wait_ge(ga.sem, ga.of(l, 4))
                A_(G[3][0:8, :], G[3][0:8, :], ACT.Ln, bias=1.0).then_inc(ga.sem, 1)
                yield from beats(4)
                act.wait_ge(gd.sem, gd.of(l, 8))
                A_(ST[64:72, :], G[6][0:8, :], ACT.Exp).then_inc(ga.sem, 1)
                act.wait_ge(gd.sem, gd.of(l, 9))
                A_(ST[96:104, :], G[7][0:8, :], ACT.Exp).then_inc(ga.sem, 1)

            def gdn_strand():
                yield from beats(10)
                for g in range(4):
                    yield from gdn(g)

            def gdn(g):
                for n, (b, a) in enumerate(((4, 6), (5, 7))):
                    act.wait_ge(nat_done.sem, nat_done.of(l, 3 * g + n + 1))
                    if g and n == 0:
                        act.wait_ge(gdn_out.sem, gdn_out.of(l, g))
                    A_(A[a], PS[:, b, :], ACT.Square).then_inc(sqn_ready.sem, 1)
                yield from beats(8)
                for n, (b, dst) in enumerate(((4, KNT(g)), (5, QNT(g)), (6, QET(g)))):
                    act.wait_ge(back_done.sem, back_done.of(l, 3 * g + n + 1))
                    A_(dst, PS[:, b, :], ACT.Copy).then_inc(back_ready.sem, 1)
                yield from beats(2)
                act.wait_ge(gm_ready.sem, gm_ready.of(l, g + 1))
                A_(A[7], A[6], ACT.Exp, scale=-1.0).then_inc(e1_ready.sem, 1)
                yield from beats(2)
                yield from beats(5)
                yield
                for j in range(1, 6):
                    act.wait_ge(x_done.sem, x_done.of(l, 6 * g + j + 1))
                    if j == 1:
                        act.wait_ge(w1_ready.sem, w1_ready.of(l, g + 1))
                        act.wait_ge(qkg_ready.sem, qkg_ready.of(l, g + 1))
                    A_(A[7], PS[:, 5, :], ACT.Copy).then_inc(xs_ready.sem, 1)
                    yield
                    yield
                act.wait_ge(u_done.sem, u_done.of(l, g + 1))
                A_(A[2], PS[:, 4, :], ACT.Copy).then_inc(u_ready.sem, 1)
                act.wait_ge(wdt_done.sem, wdt_done.of(l, g + 1))
                A_(A[3], PS[:, 5, :], ACT.Copy).then_inc(wdt_ready.sem, 1)
                act.wait_ge(wd_done.sem, wd_done.of(l, g + 1))
                A_(A[4], PS[:, 6, :], ACT.Copy).then_inc(wd_ready.sem, 1)
                yield from beats(3)
                act.wait_ge(mt_done.sem, mt_done.of(l, g + 1))
                A_(A[8][:, 0:T], PS[:, 5, T:2 * T], ACT.Copy)
                A_(A[8][:, T:2 * T], PS[:, 6, 0:T], ACT.Copy).then_inc(mt_ready.sem, 1)
                yield from beats(3)
                for n in (1, 2):
                    yield from beats(2)
                yield from beats(2)
                act.wait_ge(o_done.sem, o_done.of(l, g + 1))
                A_(A[3], PS[:, 5, :], ACT.Square).then_inc(osq_ready.sem, 1)
                A_(A[5], PS[:, 5, :], ACT.Copy, scale=PAR[:, PAR_GN:PAR_GN + 1]).then_inc(os_ready.sem, 1)
                yield
                yield from beats(2)
                yield from beats(1)

            def sb_strand():
                yield from beats(4)
                for h in range(SH):
                    act.wait_ge(sb_z_done.sem, sb_z_done.of(l, h + 1))
                    A_(SBZ, PS[:, 7, 0:384], ACT.Copy, scale=SCALE).then_inc(sb_zs.sem, 1)
                    A_(SBV[:, 0:P], PS[:, 7, 384:512], ACT.Copy).then_inc(sb_v.sem, 1)
                    act.wait_ge(sb_zs.sem, sb_zs.of(l, h + 1))
                    A_(SBE, SBZ, ACT.Abs).then_inc(sb_abs.sem, 1)
                    act.wait_ge(sb_abs.sem, sb_abs.of(l, h + 1))
                    A_(SBE, SBE, ACT.Exp, scale=-1.0).then_inc(sb_exp.sem, 1)
                    act.wait_ge(sb_exp.sem, sb_exp.of(l, h + 1))
                    A_(SBL, SBE, ACT.Ln, bias=1.0).then_inc(sb_ln.sem, 1)
                    yield from beats(3)
                    act.wait_ge(sb_y.sem, sb_y.of(l, h + 1))
                    A_(SBE, SBM, ACT.Exp).then_inc(sb_a.sem, 1)
                    A_(SBV[:, P:T], PS[:, 7, 384:512], ACT.Copy).then_inc(sb_v.sem, 1)
                    yield from beats(2)
                    act.wait_ge(sb_o_done.sem, sb_o_done.of(l, h + 1))
                    A_(SBX[:, h, :], PS[:, 7, 0:T], ACT.Copy).then_inc(sb_out.sem, 1)
                    yield

            def sw_strand():
                yield from beats(8 + 3 + 6 + 1)
                act.wait_ge(sw_vt_done.sem, sw_vt_done.of(l, 1))
                A_(SWV, PS[:, 7, :], ACT.Copy).then_inc(sw_v.sem, 1)
                yield
                for h in range(WH_):
                    act.wait_ge(sw_s.sem, sw_s.of(l, 3 * h + 3))
                    for t in range(2):
                        A_(SWP[:, t * T:(t + 1) * T], SWS[:, t * T:(t + 1) * T], ACT.Exp, bias=NM[:, t:t + 1],
                           accum_out=SUMP[:, t:t + 1]).then_inc(sw_p.sem, 1)
                    A_(SE, NM, ACT.Exp, bias=PAR[:, PAR_SK + h:PAR_SK + h + 1]).then_inc(sw_p.sem, 1)
                    yield from beats(5)
                    act.wait_ge(sw_pt_done.sem, sw_pt_done.of(l, h + 1))
                    A_(SWT, PS[:, 7, 0:384], ACT.Copy).then_inc(sw_pt.sem, 1)
                    yield
                    act.wait_ge(sw_o_done.sem, sw_o_done.of(l, h + 1))
                    A_(SWX[:, h, :], PS[:, 7, 0:T], ACT.Copy).then_inc(sw_out.sem, 1)
                    yield

            def o_hi(kg):
                src = (QKV[:, 0:4, :], SBX[:, 0:4, :], QKV[:, 4:8, :], SWX[:, 0:4, :])[kg]
                act.wait_ge(unit_used.sem, unit_used.of(l, U_IN - 3 + kg))
                if kg == 0:
                    act.wait_ge(gdn_out.sem, gdn_out.of(l, 2))
                elif kg == 1:
                    act.wait_ge(sb_out.sem, sb_out.of(l, 4))
                elif kg == 2:
                    act.wait_ge(gdn_out.sem, gdn_out.of(l, 4))
                else:
                    act.wait_ge(sw_out.sem, sw_out.of(l, 4))
                A_(XHL[:, 4 * kg:4 * kg + 4, 0:T], src, ACT.Copy).then_inc(ohi_ready.sem, 1)

            def up_pair(i, part, first=False):
                u, e, e4 = i * 8 + u_up[part], i * 8 + e_up[part], i * 6 + e_up[part] // 4 * 3
                f0 = sum(F_PARTS[:part])
                fc = i * 4 + f0
                if first:
                    splits(u_up[part], 3)
                    rstd(l, 1)
                    splits(u_up[part] + 3, 1)
                else:
                    splits(u_up[part], 4, i, 8)

                def tap0(n):
                    act.wait_ge(chunk_done.sem, chunk_done.of(l, e + (n + 1)))
                    A_(GY[:, n, :], GP[:, n, 2:2 + T], ACT.Identity,
                       scale=PAR[:, bass.ds(fc + (PAR_FCW + 2 * FC + n), 1)],
                       bias=PAR[:, bass.ds(fc + (PAR_FB + n), 1)]).then_inc(gtap0_ready.sem, 1)

                def silu(n):
                    act.wait_ge(gtap_done.sem, gtap_done.of(l, fc * 2 + (2 * n + 2)))
                    A_(GY[:, n, :], GY[:, n, :], ACT.Silu).then_inc(gsilu_done.sem, 1)

                def between(n):
                    if n:
                        tap0(n - 1)
                    if n == 3:
                        silu(0)
                tile_lo(u, e, e4, 4, between)
                tap0(3)
                splits(u_up[part] + 4, 1, i, 8)
                for n in (1, 2, 3):
                    silu(n)
                splits(u_up[part] + 5, 3, i, 8)

                def hi(n):
                    act.wait_ge(gated_done.sem, gated_done.of(l, fc + (n + 1)))
                    A_(MID[:, bass.ds(i * 4 + n, 1), 0:T], VV[:, n:n + 1, :], ACT.Copy).then_inc(
                        midhi_ready.sem, 1)

                tile_lo(u + 4, e + 4, e4 + 3, 4, lambda n: hi(n - 2) if n >= 2 else None)
                hi(2)
                hi(3)

            strands = Strands()
            for i in range(IN_TILES):
                if i == GATES_FROM:
                    strands.begin(gates_strand())
                if i == GDN_FROM:
                    strands.begin(gdn_strand())
                if i == SB_FROM:
                    strands.begin(sb_strand())
                if i == SW_FROM:
                    strands.begin(sw_strand())
                in_tile(i)
            for half in range(2):
                for n in range(4 * half, 4 * half + 4):
                    woven_splits(u_o + 2 * n, 2, lambda j: norm_tile(l, 1, n - 5) if j and n in (5, 6) else None)
                    if n == 7:
                        norm_tile(l, 1, 2)
                    tile_lo(u_o + 2 * n, e_o + 4 * n, (e_o + 4 * n) // 4 * 3, 2)
                if half == 0:
                    strands.finish()
                    o_hi(2)
                    o_hi(3)
            norm_tile(l, 1, 3)
            up_pair(0, 0, first=True)
            for part in range(2):
                with act.Fori(1 - part, F_PARTS[part] // 4) as i:
                    up_pair(i, part)
                nu = F_PARTS[part] // 4
                if part == 0:
                    with act.Fori(0, 2) as i:
                        for j in range(2):
                            u = i * (2 * nu) + (u_dn[0] + j * nu)
                            splits(u_dn[0] + j * nu, nu, i, 2 * nu)
                            tile_lo(u, i * 8 + (e_dn[0] + 4 * j), i * 6 + (e_dn[0] // 4 * 3 + 3 * j), nu)
                else:
                    for j in range(4):
                        u = u_dn[1] + j * nu
                        splits(u, 3)
                        if j:
                            norm_tile(l, 2, j - 1)
                        splits(u + 3, nu - 3)
                        tile_lo(u, e_dn[1] + 4 * j, e_dn[1] // 4 * 3 + 3 * j, nu)
                    norm_tile(l, 2, 3)

        with act.Fori(0, DEPTH) as l:
            layer(l)
        rstd(DEPTH, 0)

    @block.vector
    def _(dve):
        V = nc.vector

        def first_parts(j):
            dve.wait_ge(x_loaded[j].sem, 16)
            xw = XW0[j].rearrange("p (k t) -> p k t", k=4)
            V.tensor_tensor(xw, XT[:, 4 * j:4 * j + 4, :], NW[:, 4 * j:4 * j + 4].unsqueeze(2).to_broadcast([P, 4, T]),
                            ALU.mult).then_inc(xw_ready.sem, 1)
            dve.wait_ge(xhi_ready.sem, xhi_ready.of(0, j + 1))
            V.tensor_tensor(XHL[:, 4 * j:4 * j + 4, T:2 * T], xw, XHL[:, 4 * j:4 * j + 4, 0:T].bitcast(F32),
                            ALU.subtract).then_inc(xlo_ready.sem, 1)

        def first_sums(j):
            dve.wait_ge(sq_ready.sem, sq_ready.of(0, j + 1))
            V.tensor_reduce(PART[:, j, :], SQ0[j].rearrange("p (k t) -> p t k", k=4), AX.X, ALU.add).then_inc(
                part_ready.sem, 1)

        def norm_tile(l, n, j):
            if n == 1:
                dve.wait_ge(chunk_done.sem, chunk_done.of(l, E_IN + 16 + 4 * j + 4))
            else:
                dve.wait_ge(chunk_done.sem, chunk_done.of(l, E_LAYER - 16 + 4 * j + 4))
            dve.wait_ge(xlo_ready.sem, xlo_ready.of(l, 4 * n + j))
            w = NW[:, bass.ds(l * (2 * KC) + (n * KC + 4 * j), 4)]
            V.tensor_tensor(XW.rearrange("p (k t) -> p k t", k=4), XT[:, 4 * j:4 * j + 4, :],
                            w.unsqueeze(2).to_broadcast([P, 4, T]), ALU.mult).then_inc(xw_ready.sem, 1)
            dve.wait_ge(sq_ready.sem, sq_ready.of(l, 4 * n + j + 1))
            V.tensor_reduce(PART[:, j, :], SQ.rearrange("p (k t) -> p t k", k=4), AX.X, ALU.add).then_inc(
                part_ready.sem, 1)
            dve.wait_ge(xhi_ready.sem, xhi_ready.of(l, 4 * n + j + 1))
            V.tensor_tensor(XHL[:, 4 * j:4 * j + 4, T:2 * T], XW.rearrange("p (k t) -> p k t", k=4),
                            XHL[:, 4 * j:4 * j + 4, 0:T].bitcast(F32), ALU.subtract).then_inc(
                                xlo_ready.sem, 1)

        def rstd(l, n):
            dve.wait_ge(colsum_done.sem, colsum_done.of(l, n + 1))
            V.tensor_scalar(MS2, PS[:, 4, 0:2], 1.0 / D, EPS, ALU.mult, ALU.add).then_inc(ms_ready.sem, 1)
            dve.wait_ge(r_ready.sem, r_ready.of(l, n + 1))
            V.tensor_tensor(DIAG.rearrange("p (t c) -> p t c", t=2), IDENT.unsqueeze(1).to_broadcast([P, 2, P]),
                            R2.unsqueeze(2).to_broadcast([P, 2, P]), ALU.mult).then_inc(diag_ready.sem, 1)

        def split(u, s, h):
            dve.wait_ge(whi_ready.sem, u * 2 + (h + 1))
            k = slice(2 * h, 2 * h + 2)
            V.tensor_tensor(w_lo[:, s, k].rearrange("p k n -> p (k n)"),
                            w_raw[:, s, k].rearrange("p k n -> p (k n)"),
                            w_hi[:, s, k].rearrange("p k n -> p (k n)").bitcast(F32), ALU.subtract).then_inc(
                                wlo_ready.sem, 1)

        def split_all(u, s):
            dve.wait_ge(whi_ready.sem, u * 2 + 2)
            V.tensor_tensor(w_lo[:, s].rearrange("p k n -> p (k n)"), w_raw[:, s].rearrange("p k n -> p (k n)"),
                            w_hi[:, s].rearrange("p k n -> p (k n)").bitcast(F32), ALU.subtract).then_inc(
                                wlo_ready.sem, 2)

        dve.sem_inc(sum_ready.sem, 4)
        V.memset(SMALL, -0.5).then_inc(set_up.sem, 1)
        dve.wait_ge(nw_loaded.sem, 16)
        for j in range(AHEAD):
            first_parts(j)
            split_all(j, j)
        first_parts(2)
        first_sums(0)
        first_sums(1)
        first_parts(3)
        first_sums(2)
        first_sums(3)
        dve.wait_ge(io_loaded.sem, 16)

        def layer(l):

            def splits(u, n, i=0, step=0):
                for j in range(n):
                    v = u + AHEAD + j
                    split_all(l * U_LAYER + (i * step + v), v % SLOTS)

            def woven_splits(u, n, before=None):
                for j in range(n):
                    if before:
                        before(j)
                    v = u + AHEAD + j
                    for h in range(2):
                        split(l * U_LAYER + v, v % SLOTS, h)
                        if j < n - 1:
                            strands.beats(2)

            def add(e, n):
                dve.wait_ge(lo_ready.sem, lo_ready.of(l, e + (n + 1)))
                dve.wait_ge(chunk_done.sem, chunk_done.of(l, e + (n + 1 - 2)))
                V.tensor_tensor(SUM[:, n % 2, :], PS[:, n, 0:T], LO[:, n % 2, :], ALU.add).then_inc(
                    sum_ready.sem, 1)

            def tile_add(e, between=None):
                for n in range(4):
                    add(e, n)
                    strands.beat()
                    if between:
                        between(n)

            def wab_lo():
                dve.wait_ge(wabhi_ready.sem, wabhi_ready.of(l, 1))
                V.tensor_tensor(WABL, WABR, WABH.bitcast(F32), ALU.subtract).then_inc(wablo_ready.sem, 1)

            def in_tile(i):
                def before(j):
                    if i == 0 and j == 2:
                        rstd(l, 0)
                    elif i == 0 and j == 3:
                        wab_lo()
                    elif i == IN_TILES - 1 and j >= 2:
                        o_lo(j - 2)
                woven_splits(4 * i, 4, before)
                if i == 0:
                    dve.wait_ge(par_loaded.sem, par_loaded.of(l, 48))
                e, group, c0 = 4 * i, conv_group(IN_ORDER[i]), 4 * n_conv(i)

                def taps(n):
                    for q in range(3):
                        if q == 0:
                            dve.wait_ge(tap0_ready.sem, tap0_ready.of(l, c0 + n + 1))
                        else:
                            dve.wait_ge(tap_done.sem, tap_done.of(l, 3 * (c0 + n) + q))
                        c = PAR_GC + (2 - q) * 24 + group + n
                        V.scalar_tensor_tensor(out=CY[:, n % 2, :], in0=CV[:, n, 2 - q:2 - q + T],
                                               scalar=PAR[:, c:c + 1], in1=CY[:, n % 2, :], op0=ALU.mult,
                                               op1=ALU.add).then_inc(tap_done.sem, 1)
                def conv_strand():
                    for n in range(4):
                        taps(n)
                        yield from beats(2)

                tile_add(e)
                if group is not None:
                    strands.begin(conv_strand())

            def gates_strand():
                W = lambda k: dve.wait_ge(gd.sem, gd.of(l, k))
                yield
                dve.wait_ge(ga.sem, ga.of(l, 1))
                V.tensor_tensor(G[1][0:64, :], PS[0:64, 4, 0:T], G[0][0:64, :], ALU.add).then_inc(gd.sem, 1)
                W(1)
                V.tensor_tensor(G[2][0:64, :], G[1][0:64, :], RSTD[0:64, :], ALU.mult).then_inc(gd.sem, 1)
                W(2)
                V.tensor_scalar(G[5][0:8, :], G[2][0:8, :], GPAR[0:8, 1:2], 0.0, ALU.add, ALU.max).then_inc(
                    gd.sem, 1)
                yield from beats(4)
                dve.wait_ge(ga.sem, ga.of(l, 5))
                V.tensor_tensor(G[5][0:8, :], G[5][0:8, :], G[3][0:8, :], ALU.add).then_inc(gd.sem, 1)
                W(4)
                V.tensor_scalar(G[5][0:8, :], G[5][0:8, :], EXPA[0:8, :], -1.0, ALU.mult, ALU.mult).then_inc(
                    gd.sem, 1)
                V.tensor_scalar(G[4][32:40, :], G[4][32:40, :], 1.0, None, ALU.add).then_inc(gd.sem, 1)
                W(6)
                dve.wait_ge(pads_ready.sem, pads_ready.of(l, 1))
                V.reciprocal(ST[32:40, :], G[4][32:40, :]).then_inc(gd.sem, 1)
                V.tensor_tensor_scan(G[6][0:8, :], con["reset"][0:8, :], G[5][0:8, :], 0.0, ALU.mult,
                                     ALU.add).then_inc(gd.sem, 1)
                W(8)
                g3 = G[6][0:8, :].rearrange("p (n c) -> p n c", c=CH)
                V.tensor_tensor(G[7][0:8, :].rearrange("p (n c) -> p n c", c=CH),
                                g3[:, :, CH - 1:CH].to_broadcast([8, 4, CH]), g3, ALU.subtract).then_inc(
                                    gd.sem, 1)
                V.tensor_scalar(ST[0:8, :], G[6][0:8, :], -1.0, None, ALU.mult).then_inc(gd.sem, 1)
                yield from beats(8)
                dve.wait_ge(gate_t_done.sem, gate_t_done.of(l, 1))
                V.tensor_copy(COL, PS[:, 6, 0:T].rearrange("p (t r) -> p t r", t=2)).then_inc(
                    gate_cols_ready.sem, 1)
                dve.wait_ge(dec_done.sem, dec_done.of(l, 1))
                V.tensor_copy(DEC, PS[:, 7, 0:32]).then_inc(gate_cols_ready.sem, 1)
                dve.wait_ge(gate_cols_ready.sem, gate_cols_ready.of(l, 1))
                V.tensor_tensor(BE, COL[:, :, 32:40], COL[:, :, 64:72], ALU.mult).then_inc(
                    gate_cols_ready.sem, 1)

            def gdn_strand():
                yield from beats(10)
                for g in range(4):
                    yield from gdn(g)

            def gdn(g):
                hh = 2 * g
                for n, a in enumerate((6, 7)):
                    dve.wait_ge(sqn_ready.sem, sqn_ready.of(l, 2 * g + n + 1))
                    V.tensor_reduce(SS[:, 4 * n:4 * n + 4], b4(A[a]), AX.X, ALU.add).then_inc(ss_ready.sem, 1)
                dve.wait_ge(ss_ready.sem, ss_ready.of(l, 3 * g + 2))
                V.tensor_scalar(SS, SS, EPS, None, ALU.add).then_inc(ss_ready.sem, 1)
                dve.wait_ge(nat_done.sem, nat_done.of(l, 3 * g + 3))
                V.tensor_tensor(b22(A[2]), b22(PS[:, 6, :]),
                                COL[:, :, 32 + hh:34 + hh].unsqueeze(3).to_broadcast([P, 2, 2, P]),
                                ALU.mult).then_inc(nat_ready.sem, 1)
                yield from beats(3)
                for n, (a, b, c, need) in enumerate(((0, 4, 1, 1), (3, 4, 0, 1), (1, 4, 2, 2), (4, 5, 3, 3),
                                                     (5, 5, 4, 4))):
                    dve.wait_ge(co_ready.sem, co_ready.of(l, 4 * g + need))
                    f_ = RR[:, 0:4] if c == 0 else CO[:, c - 1, :]
                    V.tensor_tensor(b4(A[a]), b4(PS[:, b, :]), tb(f_), ALU.mult).then_inc(nat_ready.sem, 1)
                    yield
                yield from beats(2)
                dve.wait_ge(grow_done.sem, grow_done.of(l, g + 1))
                for t in range(2):
                    for i in range(2):
                        r = V.scalar_tensor_tensor(out=A[6][:, blk(t, i)], in0=PS[:, 6, blk(t, i)],
                                                   scalar=COL[:, t, hh + i:hh + i + 1], in1=con["gmask"],
                                                   op0=ALU.subtract, op1=ALU.max)
                r.then_inc(gm_ready.sem, 1)
                yield from beats(2)
                dve.wait_ge(e1_ready.sem, e1_ready.of(l, g + 1))
                dve.wait_ge(qk_done.sem, qk_done.of(l, g + 1))
                V.tensor_tensor(A[9], PS[:, 5, :], A[7], ALU.mult).then_inc(qkg_ready.sem, 1)
                dve.wait_ge(beta_done.sem, beta_done.of(l, g + 1))
                V.tensor_tensor(A[6], PS[:, 6, :], A[7], ALU.mult).then_inc(w1_ready.sem, 1)
                dve.wait_ge(kk_done.sem, kk_done.of(l, g + 1))
                dve.wait_ge(w1_ready.sem, w1_ready.of(l, g + 1))
                V.tensor_tensor(A[3], PS[:, 4, :], A[6], ALU.mult).then_inc(at_ready.sem, 1)
                yield from beats(5)
                dve.wait_ge(x_done.sem, x_done.of(l, 6 * g + 1))
                V.tensor_tensor(b4(A[4]), IDENT.unsqueeze(1).to_broadcast([P, 4, P]), b4(PS[:, 4, :]),
                                ALU.subtract).then_inc(d_ready.sem, 1)
                yield
                for j in range(1, 6):
                    yield
                    if j < 5:
                        dve.wait_ge(dx_done.sem, dx_done.of(l, 4 * g + j))
                        V.tensor_tensor(A[4], A[4], PS[:, 4, :], ALU.subtract).then_inc(d_ready.sem, 1)
                    dve.wait_ge(ex_done.sem, ex_done.of(l, 5 * g + j))
                    if j == 1:
                        dve.wait_ge(e0_ready.sem, e0_ready.of(l, g + 1))
                    V.tensor_tensor(A[5], A[5], PS[:, 6, :], ALU.subtract).then_inc(e_ready.sem, 1)
                    yield
                yield from beats(3)
                dve.wait_ge(kv_done.sem, kv_done.of(l, g + 1))
                V.tensor_copy(S_[1], PS[:, 4, 0:2 * P]).then_inc(s_ready.sem, 1)
                yield from beats(3)
                for n in (1, 2):
                    kvu = PS[:, 5, 0:2 * P] if n == 1 else PS[:, 4, 2 * P:4 * P]
                    dve.wait_ge(s_ready.sem, s_ready.of(l, 3 * g + n))
                    for i in range(2):
                        c = slice(i * P, (i + 1) * P)
                        r = V.scalar_tensor_tensor(out=S_[n + 1][:, c], in0=S_[n][:, c],
                                                   scalar=DEC[:, 4 * (hh + i) + n:4 * (hh + i) + n + 1],
                                                   in1=kvu[:, c], op0=ALU.mult, op1=ALU.add)
                    r.then_inc(ds_ready.sem, 1)
                    dve.wait_ge(mst_done.sem, mst_done.of(l, 2 * g + n))
                    dve.wait_ge(ds_ready.sem, ds_ready.of(l, 2 * g + n))
                    V.tensor_tensor(S_[n + 1], S_[n + 1], PS[:, 6, 0:2 * P], ALU.subtract).then_inc(s_ready.sem, 1)
                    yield from beats(2)
                dve.wait_ge(ws_done.sem, ws_done.of(l, g + 1))
                v = A[2][CH:P, 0:2 * P]
                V.tensor_tensor(v, v, PS[CH:P, 4, 0:2 * P], ALU.subtract)
                v = A[2][:, 2 * P:4 * P]
                V.tensor_tensor(v, v, PS[:, 4, 2 * P:4 * P], ALU.subtract).then_inc(v_ready.sem, 1)
                yield from beats(2)
                yield
                dve.wait_ge(osum_done.sem, osum_done.of(l, g + 1))
                V.tensor_scalar(MSO, PS[:, 6, 0:4], 1.0 / P, EPS, ALU.mult, ALU.add).then_inc(mso_ready.sem, 1)
                dve.wait_ge(ro_ready.sem, ro_ready.of(l, g + 1))
                V.tensor_tensor(b4(A[4]), IDENT.unsqueeze(1).to_broadcast([P, 4, P]), tb(RO),
                                ALU.mult).then_inc(odiag_ready.sem, 1)
                yield from beats(2)
                dve.wait_ge(orow_done.sem, orow_done.of(l, g + 1))
                dve.wait_ge(oz_ready.sem, oz_ready.of(l, g + 1))
                V.tensor_tensor(pair(QKV, hh), b22(A[5]), b22(PS[:, 4, :]), ALU.mult).then_inc(gdn_out.sem, 1)
                yield from beats(1)

            def sb_strand():
                yield from beats(4)
                for h in range(SH):
                    dve.wait_ge(sb_ln.sem, sb_ln.of(l, h + 1))
                    V.scalar_tensor_tensor(out=SBL, in0=SBZ, scalar=0.0, in1=SBL,
                                           op0=ALU.max, op1=ALU.add).then_inc(sb_sp.sem, 1)
                    dve.wait_ge(sb_sp.sem, sb_sp.of(l, 2 * h + 1))
                    V.tensor_tensor(SBL, SBL, con["sbmask"], ALU.mult).then_inc(sb_sp.sem, 1)
                    yield from beats(3)
                    dve.wait_ge(sb_c_done.sem, sb_c_done.of(l, h + 1))
                    dve.wait_ge(sb_zm.sem, sb_zm.of(l, h + 1))
                    V.tensor_tensor(SBM, SBM, PS[:, 7, 0:384], ALU.add).then_inc(sb_y.sem, 1)
                    yield from beats(2)
                    yield

            def sw_strand():
                yield from beats(8)
                for c in range(3):
                    x = SWX[:, 2 * c:2 * c + 2, :]
                    dve.wait_ge(rot_done.sem, rot_done.of(l, c + 1))
                    if c:
                        dve.wait_ge(roped.sem, roped.of(l, c))
                    V.tensor_tensor(SWP.rearrange("p (a t) -> p a t", a=2),
                                    PS[:, 7, :].rearrange("p (a t) -> p a t", a=2),
                                    con["sin"].unsqueeze(1).to_broadcast([P, 2, T]), ALU.mult).then_inc(xsin.sem, 1)
                    dve.wait_ge(xsin.sem, xsin.of(l, c + 1))
                    dve.wait_ge(xcos.sem, xcos.of(l, c + 1))
                    V.tensor_tensor(x, SWS.rearrange("p (a t) -> p a t", a=2),
                                    SWP.rearrange("p (a t) -> p a t", a=2), ALU.add).then_inc(roped.sem, 1)
                    yield from beats((3, 6, 1)[c])
                yield
                for h in range(WH_):
                    dve.wait_ge(sw_s_done.sem, sw_s_done.of(l, h + 1))
                    if h:
                        dve.wait_ge(sw_den.sem, sw_den.of(l, 3 * h))
                    V.scalar_tensor_tensor(out=SWS, in0=PS[:, 7, :], scalar=SCALE, in1=con["swaadd"],
                                           op0=ALU.mult, op1=ALU.add).then_inc(sw_s.sem, 1)
                    dve.wait_ge(sw_s.sem, sw_s.of(l, 3 * h + 1))
                    V.tensor_reduce(MX, SWS.rearrange("p (t k) -> p t k", t=2), AX.X, ALU.max).then_inc(sw_s.sem, 1)
                    dve.wait_ge(sw_s.sem, sw_s.of(l, 3 * h + 2))
                    V.tensor_scalar(NM, MX, PAR[:, PAR_SK + h:PAR_SK + h + 1], -1.0, ALU.max, ALU.mult).then_inc(
                        sw_s.sem, 1)
                    yield
                    dve.wait_ge(sw_p.sem, sw_p.of(l, 3 * h + 3))
                    V.tensor_tensor(DEN, SUMP, SE, ALU.add).then_inc(sw_den.sem, 1)
                    dve.wait_ge(sw_den.sem, sw_den.of(l, 3 * h + 1))
                    V.reciprocal(REC, DEN).then_inc(sw_den.sem, 1)
                    dve.wait_ge(sw_den.sem, sw_den.of(l, 3 * h + 2))
                    p3 = SWP.rearrange("p (t k) -> p t k", t=2)
                    V.tensor_tensor(p3, p3, REC.unsqueeze(2).to_broadcast([P, 2, T]), ALU.mult).then_inc(
                        sw_den.sem, 1)
                    yield from beats(4)
                    yield
                    yield

            def o_lo(kg):
                src = (QKV[:, 0:4, :], SBX[:, 0:4, :], QKV[:, 4:8, :], SWX[:, 0:4, :])[kg]
                dve.wait_ge(ohi_ready.sem, ohi_ready.of(l, kg + 1))
                V.tensor_tensor(XHL[:, 4 * kg:4 * kg + 4, T:2 * T], src,
                                XHL[:, 4 * kg:4 * kg + 4, 0:T].bitcast(F32), ALU.subtract).then_inc(
                                    olo_ready.sem, 1)

            def up_pair(i, part, first=False):
                u, e = i * 8 + u_up[part], i * 8 + e_up[part]
                f0 = sum(F_PARTS[:part])
                fc = i * 4 + f0
                if first:
                    splits(u_up[part], 2)
                    rstd(l, 1)
                    splits(u_up[part] + 2, 2)
                else:
                    splits(u_up[part], 4, i, 8)

                def taps(n):
                    for q in range(2):
                        if q == 0:
                            dve.wait_ge(gtap0_ready.sem, gtap0_ready.of(l, fc + (n + 1)))
                        else:
                            dve.wait_ge(gtap_done.sem, gtap_done.of(l, fc * 2 + (2 * n + 1)))
                        V.scalar_tensor_tensor(out=GY[:, n, :], in0=GP[:, n, 1 - q:1 - q + T],
                                               scalar=PAR[:, bass.ds(fc + (PAR_FCW + (1 - q) * FC + n), 1)],
                                               in1=GY[:, n, :], op0=ALU.mult, op1=ALU.add).then_inc(
                                                   gtap_done.sem, 1)
                tile_add(e, lambda n: taps(n - 2) if n >= 2 else None)
                splits(u_up[part] + 4, 1, i, 8)
                taps(2)
                taps(3)
                splits(u_up[part] + 5, 3, i, 8)

                def low(n):
                    dve.wait_ge(midhi_ready.sem, midhi_ready.of(l, fc + (n + 1)))
                    V.tensor_tensor(MID[:, bass.ds(i * 4 + n, 1), T:2 * T], VV[:, n:n + 1, :],
                                    MID[:, bass.ds(i * 4 + n, 1), 0:T].bitcast(F32), ALU.subtract).then_inc(
                                        midlo_ready.sem, 1)
                tile_add(e + 4, lambda n: low(0) if n == 3 else None)
                for n in (1, 2, 3):
                    low(n)

            strands = Strands()
            for i in range(IN_TILES):
                if i == GATES_FROM:
                    strands.begin(gates_strand())
                if i == GDN_FROM:
                    strands.begin(gdn_strand())
                if i == SB_FROM:
                    strands.begin(sb_strand())
                if i == SW_FROM:
                    strands.begin(sw_strand())
                in_tile(i)
            for half in range(2):
                for n in range(4 * half, 4 * half + 4):
                    woven_splits(u_o + 2 * n, 2, lambda j: norm_tile(l, 1, n - 5) if j and n in (5, 6) else None)
                    if n == 7:
                        norm_tile(l, 1, 2)
                    tile_add(e_o + 4 * n)
                if half == 0:
                    strands.finish()
                    o_lo(2)
                    o_lo(3)
            norm_tile(l, 1, 3)
            up_pair(0, 0, first=True)
            for part in range(2):
                with dve.Fori(1 - part, F_PARTS[part] // 4) as i:
                    up_pair(i, part)
                nu = F_PARTS[part] // 4
                if part == 0:
                    with dve.Fori(0, 2) as i:
                        for j in range(2):
                            splits(u_dn[0] + j * nu, nu, i, 2 * nu)
                            tile_add(i * 8 + (e_dn[0] + 4 * j))
                else:
                    for j in range(4):
                        splits(u_dn[1] + j * nu, 3)
                        if j:
                            norm_tile(l, 2, j - 1)
                        splits(u_dn[1] + j * nu + 3, nu - 3)
                        tile_add(e_dn[1] + 4 * j)
                    norm_tile(l, 2, 3)

        with dve.Fori(0, DEPTH) as l:
            layer(l)
        rstd(DEPTH, 0)
        x4 = XT[:, KC - 4:KC, :]
        V.tensor_tensor(x4, x4, NW[:, NORMS * KC - 4:NORMS * KC].unsqueeze(2).to_broadcast([P, 4, T]),
                        ALU.mult).then_inc(last_xw.sem, 1)
        dve.wait_ge(rstd_ready.sem, rstd_ready.of(DEPTH, 1))
        dve.wait_ge(fin_xw.sem, 3)
        dve.wait_ge(last_xw.sem, 1)
        for j in range(4):
            x4 = XT[:, 4 * j:4 * j + 4, :]
            V.tensor_tensor(x4, x4, RSTD.unsqueeze(1).to_broadcast([P, 4, T]), ALU.mult).then_inc(fin_y.sem, 1)

    @block.gpsimd
    def _(pool):
        Q = nc.gpsimd

        pool.sem_inc(chunk_done.sem, 2)
        pool.wait_ge(io_loaded.sem, 16)

        def power(dst, src, n, done):
            Q.tensor_tensor(dst, src, MHALF[:, 0:n], ALU.pow).then_inc(done, 1)

        def layer(l):

            def finish(e, n, dst):
                pool.wait_ge(sum_ready.sem, sum_ready.of(l, e + (n + 1)))
                Q.tensor_tensor(dst, SUM[:, n % 2, :], RSTD, ALU.mult).then_inc(chunk_done.sem, 1)

            def residual(e, n, x):
                pool.wait_ge(sum_ready.sem, sum_ready.of(l, e + (n + 1)))
                Q.tensor_tensor(x, x, SUM[:, n % 2:n % 2 + 1, :], ALU.add).then_inc(chunk_done.sem, 1)

            Q.dma_start(PAR[:, 0:PAR_N], params[bass.ds(l, 1)].rearrange("a p n -> p (a n)")).then_inc(
                par_loaded.sem, 16)
            Q.dma_start(GPAR[0:8, 0:2], gate_par[bass.ds(l, 1)].rearrange("a p n -> p (a n)")).then_inc(
                par_loaded.sem, 16)
            Q.dma_start(WABR, wab[bass.ds(l, 1)].rearrange("a p k n -> p (a k) n")).then_inc(wab_loaded.sem, 16)
            Q.dma_start(CON, consts).then_inc(par_loaded.sem, 16)
            Q.memset(ST, 0.0).then_inc(pads_ready.sem, 1)
            Q.memset(CV[:, :, 0:3], 0.0)
            pool.wait_ge(ms_ready.sem, ms_ready.of(l, 1))
            power(R2, MS2, 2, r_ready.sem)

            def gdn_strand():
                yield from beats(10)
                for g in range(4):
                    yield from gdn(g)

            def gdn(g):
                hh = 2 * g
                rk, rq = RR[:, 0:4], RR[:, 4:8]
                r3 = lambda a: a.rearrange("p (t i) -> p t i", t=2)
                pool.wait_ge(ss_ready.sem, ss_ready.of(l, 3 * g + 3))
                if g:
                    pool.wait_ge(gdn_out.sem, gdn_out.of(l, g))
                power(RR, SS, 8, rr_ready.sem)
                pool.wait_ge(rr_ready.sem, rr_ready.of(l, g + 1))
                if g == 0:
                    pool.wait_ge(gate_cols_ready.sem, gate_cols_ready.of(l, 3))
                Q.tensor_tensor(r3(CO[:, 0, :]), r3(rk), BE[:, :, hh:hh + 2], ALU.mult).then_inc(co_ready.sem, 1)
                Q.tensor_tensor(r3(CO[:, 1, :]), r3(rk), COL[:, :, 96 + hh:98 + hh], ALU.mult).then_inc(
                    co_ready.sem, 1)
                Q.tensor_scalar(CO[:, 2, :], rq, SCALE, None, ALU.mult).then_inc(co_ready.sem, 1)
                pool.wait_ge(co_ready.sem, co_ready.of(l, 4 * g + 3))
                Q.tensor_tensor(r3(CO[:, 3, :]), r3(CO[:, 2, :]), COL[:, :, 64 + hh:66 + hh], ALU.mult).then_inc(
                    co_ready.sem, 1)
                yield from beats(8 + 2 + 2)
                pool.wait_ge(at_ready.sem, at_ready.of(l, g + 1))
                for j in range(6):
                    bt = A[8] if j % 2 == 0 else A[6]
                    if j >= 2:
                        pool.wait_ge(x_done.sem, x_done.of(l, 6 * g + j - 1))
                        pool.wait_ge(e0_ready.sem, e0_ready.of(l, g + 1))
                    Q.tensor_tensor(b4(bt), b4(A[3]),
                                    con["level"][:, j * P:(j + 1) * P].unsqueeze(1).to_broadcast([P, 4, P]),
                                    ALU.mult).then_inc(bt_ready.sem, 1)
                    if j == 0:
                        pool.wait_ge(bt_ready.sem, bt_ready.of(l, 6 * g + 1))
                        Q.tensor_tensor(b4(A[5]), IDENT.unsqueeze(1).to_broadcast([P, 4, P]), b4(A[8]),
                                        ALU.subtract).then_inc(e0_ready.sem, 1)
                    else:
                        yield from beats((6, 2, 2, 2, 2)[j - 1])
                yield from beats(2)
                yield from beats(3 + 3 + 4 + 2)
                pool.wait_ge(os_ready.sem, os_ready.of(l, g + 1))
                pool.wait_ge(silu_done.sem, silu_done.of(l, 4 * n_silu(4 if g < 2 else 11)))
                Q.tensor_tensor(b22(A[5]), b22(A[5]), pair(Z, hh), ALU.mult).then_inc(oz_ready.sem, 1)
                yield
                pool.wait_ge(mso_ready.sem, mso_ready.of(l, g + 1))
                power(RO, MSO, 4, ro_ready.sem)
                yield from beats(2)
                yield from beats(1)

            def sb_strand():
                yield from beats(4)
                for h in range(SH):
                    pool.wait_ge(sb_zs.sem, sb_zs.of(l, h + 1))
                    if h:
                        pool.wait_ge(sb_a.sem, sb_a.of(l, h))
                    Q.tensor_tensor(SBM, SBZ, con["sbadd"], ALU.add).then_inc(sb_zm.sem, 1)
                    yield from beats(3)
                    yield from beats(2)
                    yield

            def sw_strand():
                yield from beats(8)
                for c in range(3):
                    if c:
                        pool.wait_ge(roped.sem, roped.of(l, c))
                    else:
                        pool.wait_ge(sb_out.sem, sb_out.of(l, 4))
                    pool.wait_ge(chunk_done.sem, chunk_done.of(l, 48 if c < 2 else 52))
                    Q.tensor_tensor(SWS.rearrange("p (a t) -> p a t", a=2), SWX[:, 2 * c:2 * c + 2, :],
                                    con["cos"].unsqueeze(1).to_broadcast([P, 2, T]), ALU.mult).then_inc(xcos.sem, 1)
                    yield from beats((3, 6, 1)[c])

            strands = Strands()
            for i in range(IN_TILES):
                if i == GDN_FROM:
                    strands.begin(gdn_strand())
                if i == SB_FROM:
                    strands.begin(sb_strand())
                if i == SW_FROM:
                    strands.begin(sw_strand())
                strands.beats(12)
                name, e = IN_ORDER[i], 4 * i
                for n in range(4):
                    if conv_group(name) is not None:
                        if i:
                            pool.wait_ge(tap_done.sem, tap_done.of(l, 3 * (4 * n_conv(i) - 4 + n) + 3))
                        dst = CV[:, n, 3:3 + T]
                    elif name[0] == "z":
                        dst = Z[:, 4 * int(name[1]) + n, :]
                    elif name[:2] == "sb":
                        dst = SBX[:, 4 * int(name[2]) + n, :]
                    else:
                        dst = SWX[:, 4 * int(name[2]) + n, :]
                        pool.wait_ge(silu_done.sem, silu_done.of(l, 4 * n_silu(IN_TILES)))
                    finish(e, n, dst)
                    strands.beat()
            for half in range(2):
                for n8 in range(4 * half, 4 * half + 4):
                    strands.beats(4)
                    for n in range(4):
                        c = 4 * (n8 % 4) + n
                        residual(e_o + 4 * n8, n, XT[:, c:c + 1, :])
                        strands.beat()
                strands.finish()
            pool.wait_ge(olo_ready.sem, olo_ready.of(l, 4))
            zeros = IDENT[:, 0:8].rearrange("p (s c) -> p s c", s=4)
            Q.tensor_tensor(GP[:, :, 0:2], zeros, zeros, ALU.subtract)
            pool.wait_ge(ms_ready.sem, ms_ready.of(l, 2))
            power(R2, MS2, 2, r_ready.sem)
            for part in range(2):
                with pool.Fori(0, F_PARTS[part] // 4) as i:
                    e = i * 8 + e_up[part]
                    fc = i * 4 + sum(F_PARTS[:part])
                    pool.wait_ge(rstd_ready.sem, rstd_ready.of(l, 2))
                    for n in range(4):
                        finish(e, n, GP[:, n, 2:2 + T])
                    for n in range(4):
                        pool.wait_ge(sum_ready.sem, sum_ready.of(l, e + (4 + n + 1)))
                        Q.tensor_tensor(VV[:, n, :], SUM[:, n % 2, :], RSTD, ALU.mult).then_inc(
                            chunk_done.sem, 1)
                        pool.wait_ge(chunk_done.sem, chunk_done.of(l, e + (4 + n + 1)))
                        pool.wait_ge(gsilu_done.sem, gsilu_done.of(l, fc + (n + 1)))
                        Q.tensor_tensor(VV[:, n, :], VV[:, n, :], GY[:, n, :], ALU.mult).then_inc(
                            gated_done.sem, 1)
                if part == 0:
                    with pool.Fori(0, 2) as i:
                        for j in range(2):
                            for n in range(4):
                                residual(i * 8 + (e_dn[0] + 4 * j), n, XT[:, bass.ds(i * 8 + (4 * j + n), 1), :])
                else:
                    for j in range(4):
                        for n in range(4):
                            residual(e_dn[1] + 4 * j, n, XT[:, 4 * j + n:4 * j + n + 1, :])

        with pool.Fori(0, DEPTH) as l:
            layer(l)
        for j in range(3):
            pool.wait_ge(sq_ready.sem, sq_ready.of(DEPTH, j + 1))
            pool.wait_ge(xw_ready.sem, xw_ready.of(DEPTH, j + 1))
            x4 = XT[:, 4 * j:4 * j + 4, :]
            k = NORMS * KC - KC + 4 * j
            Q.tensor_tensor(x4, x4, NW[:, k:k + 4].unsqueeze(2).to_broadcast([P, 4, T]), ALU.mult).then_inc(
                fin_xw.sem, 1)
        pool.wait_ge(ms_ready.sem, ms_ready.of(DEPTH, 1))
        power(R2, MS2, 2, r_ready.sem)

    block.__exit__(None, None, None)


def _unit(w):
    return w.reshape(4, 128, 512).transpose(1, 0, 2).reshape(128, 2048)


def _shape_constants():
    import numpy as np
    c = {}
    i = np.arange(128)
    rot = np.zeros((128, 128), np.float32)
    rot[i[64:], i[:64]] = -1.0
    rot[i[:64], i[64:]] = 1.0
    c["rot"] = rot
    c["negu"] = -(i[:, None] >= i[None, :]).astype(np.float32)
    c["negone"] = -np.ones((128, 128), np.float32)
    up = (i[None, :] > i[:, None]).astype(np.float32)
    c["sbmask"] = np.concatenate([up, np.ones((128, 128), np.float32), up], 1)
    c["sbadd"] = np.where(c["sbmask"] > 0, 0.0, -1e30).astype(np.float32)
    half = 64
    inv = np.float32(10000.0) ** (-np.arange(half, dtype=np.float32) / np.float32(half))
    ang = (np.arange(256, dtype=np.float32)[:, None] * inv[None, :].astype(np.float32)).astype(np.float32)
    c["cos"] = np.tile(np.cos(ang).T, (2, 1)).astype(np.float32)
    c["sin"] = np.tile(np.sin(ang).T, (2, 1)).astype(np.float32)
    q = np.arange(128)
    k = np.arange(256)
    m = []
    for t in range(2):
        nq, nk = (2 * t + q // 64)[:, None], (k // 64)[None, :]
        m.append(np.where((nk == nq) | (nk == nq - 1), 0.0, -1e30))
    c["swaadd"] = np.concatenate(m, 1).astype(np.float32)
    same = (i[:, None] // 64 == i[None, :] // 64)
    c["gmask"] = np.where(same & (i[None, :] >= i[:, None]), 0.0, 1e30).astype(np.float32)
    lev = []
    for j in range(6):
        b = 2 ** j
        lev.append(((i[:, None] // (2 * b) == i[None, :] // (2 * b)) & (i[:, None] // b % 2 == 0)
                    & (i[None, :] // b % 2 == 1)).astype(np.float32))
    c["level"] = np.concatenate(lev, 1)
    c["reset"] = np.tile((np.arange(256) % 64 != 0).astype(np.float32), (128, 1))
    return np.ascontiguousarray(np.concatenate([c[n] for n in CONST], 1))


def _layout(a):
    import numpy as np
    units = np.zeros((U_ALL + SLOTS, 128, 2048), np.float32)
    wab = np.zeros((DEPTH, 128, 16, 64), np.float32)
    par = np.zeros((DEPTH, 128, PAR_N), np.float32)
    cols = {"q0": 1536, "k0": 2560, "v0": 3584, "q1": 2048, "k1": 3072, "v1": 4096, "z0": 4608, "z1": 5120,
            "sb0": 0, "sb1": 512, "sb2": 1024, "sw0": 5648, "sw1": 6160}
    in_cols = [cols[n] for n in IN_ORDER]
    for l in range(DEPTH):
        u = l * U_LAYER
        for c in in_cols:
            for k in range(4):
                units[u] = _unit(a["w_in"][l, k * 512:(k + 1) * 512, c:c + 512])
                u += 1
        k_rows = [512, 0, 1024, 1536]
        for half in range(2):
            for n in range(4):
                for k in k_rows[2 * half:2 * half + 2]:
                    units[u] = _unit(a["w_o"][l, k:k + 512, n * 512:(n + 1) * 512])
                    u += 1
        f0 = 0
        for part in F_PARTS:
            for i in range(part // 4):
                for base in (0, DFF):
                    c = base + (f0 + 4 * i) * 128
                    for k in range(4):
                        units[u] = _unit(a["w_up"][l, k * 512:(k + 1) * 512, c:c + 512])
                        u += 1
            for n in range(4):
                for k in range(part // 4):
                    r = (f0 + 4 * k) * 128
                    units[u] = _unit(a["w_down"][l, r:r + 512, n * 512:(n + 1) * 512])
                    u += 1
            f0 += part
        ab = a["w_in"][l, :, 5632:5648].reshape(16, 128, 16).transpose(1, 0, 2)
        wab[l, :, :, 0:8] = ab[:, :, 0:8]
        wab[l, :, :, 32:40] = ab[:, :, 8:16]
        par[l, :, PAR_GC:PAR_GC + 96] = a["gdn_conv"][l].reshape(96, 128).T
        par[l, :, PAR_FCW:PAR_FCW + 132] = a["ffn_conv"][l].reshape(132, 128).T
        par[l, :, PAR_FB:PAR_FB + 44] = a["ffn_conv_bias"][l].reshape(44, 128).T
        par[l, :, PAR_GN] = a["gdn_norm"][l]
        par[l, :, PAR_SK:PAR_SK + 4] = a["swa_sinks"][l][None, :]
    gate = np.stack([a["gdn_a_log"], a["gdn_dt_bias"]], 2)
    x = np.ascontiguousarray(a["x"][0].T.reshape(16, 128, 256).transpose(1, 0, 2))
    io = np.concatenate([np.eye(128, dtype=np.float32), np.ones((128, 128), np.float32)], 1)
    norms = [a[n][l] for l in range(DEPTH) for n in ("attn_norm", "ffn_norm")] + [a["final_norm"]]
    nw = np.ascontiguousarray(np.concatenate([w.reshape(16, 128).T for w in norms], 1))
    return {"units": units, "wab": wab, "params": par, "gate_par": np.ascontiguousarray(gate),
            "consts": _shape_constants(), "ident_ones": io, "x_in": x, "norm_w": nw}


def kernel(**inputs):
    import numpy as np
    import concourse.bacc as bacc
    from concourse.bass_utils import run_bass_kernel_spmd

    arrays = _layout({k: np.asarray(v) for k, v in inputs.items()})
    nc = bacc.Bacc("TRN2", target_bir_lowering=False, num_devices=1)
    aps = {n: nc.dram_tensor(n, a.shape, F32, kind="ExternalInput").ap() for n, a in arrays.items()}
    out = nc.dram_tensor("out", (128, 16, 256), F32, kind="ExternalOutput").ap()
    build(nc, **aps, out=out)
    r = run_bass_kernel_spmd(nc, [arrays], core_ids=[0])
    y = r.results[0]["out"]
    return y.transpose(1, 0, 2).reshape(2048, 256).T.reshape(1, 256, 2048)
```

```python
import concourse.bass as bass
from concourse import mybir

F32 = mybir.dt.float32
F32R = mybir.dt.float32r
ACT = mybir.ActivationFunctionType
ALU = mybir.AluOpType
AX = mybir.AxisListType

P = 128
D = 2048
T = 256
DEPTH = 2
KC = D // P
GH, SH, WH_, KVH = 8, 4, 4, 2
CH = 64
DFF = 5632
FC = DFF // P
F_PARTS = (24, 20)
SCALE = float(P) ** -0.5
EPS = 1e-6
NORMS = 2 * DEPTH + 1
AHEAD = 2
SLOTS = 4

IN_ORDER = ["q0", "k0", "v0", "z0", "q1", "k1", "v1", "sb0", "sb1", "sb2", "z1", "sw0", "sw1"]
IN_TILES = len(IN_ORDER)
U_IN = IN_TILES * 4
U_O = 16
U_UP = [F_PARTS[0] // 4 * 8, F_PARTS[1] // 4 * 8]
U_DN = [F_PARTS[0] // 4 * 4, F_PARTS[1] // 4 * 4]
U_LAYER = U_IN + U_O + sum(U_UP) + sum(U_DN)
U_ALL = DEPTH * U_LAYER
E_IN, E_O = IN_TILES * 4, 32
E_UP = [F_PARTS[0] * 2, F_PARTS[1] * 2]
E_DN = [16, 16]
E_LAYER = E_IN + E_O + sum(E_UP) + sum(E_DN)

PAR_GC, PAR_FCW, PAR_FB, PAR_GN, PAR_SK, PAR_N = 0, 96, 228, 272, 273, 277

CONST = {"rot": 128, "negu": 128, "negone": 128, "sbmask": 384, "sbadd": 384, "cos": 256, "sin": 256,
         "swaadd": 512, "gmask": 128, "level": 768, "reset": 256}
CONST_AT, _at = {}, 0
for _n, _w in CONST.items():
    CONST_AT[_n] = _at
    _at += _w
CONST_N = _at


class Signal:

    def __init__(self, sem, per_layer, before):
        self.sem, self.per_layer, self.before = sem, per_layer, before

    def of(self, l, k):
        return l * self.per_layer + (self.before + k)


GATES_FROM, GDN_FROM, SB_FROM, SW_FROM = 1, 3, 10, 12

GDN_START = 8
GDN_BEATS = {"keys": 4, "values": 3, "back": 2, "products": 2, "beta": 5, "transpose": 2, "x": 1, "e": 1, "u": 3,
             "kv": 3, "state": 2, "ws": 2, "out": 1, "sums": 2, "rows": 1}
SB_BEATS = (3, 2, 2)
SW_BEATS = (5, 1, 1)


def beats(n):
    for _ in range(n):
        yield


class Strands:

    def __init__(self):
        self.running = []

    def begin(self, strand):
        self.running.append(strand)

    def beat(self):
        for strand in self.running:
            next(strand, None)

    def beats(self, n):
        for _ in range(n):
            self.beat()

    def finish(self):
        for strand in self.running:
            for _ in strand:
                pass
        self.running = []


def build(nc, units, wab, params, gate_par, consts, ident_ones, x_in, norm_w, out):
    off = [16512]

    def place(name, cols, dt=F32, at=None):
        if at is None:
            at = off[0]
            off[0] += cols * 4
        return nc.alloc_sbuf_tensor_at(name, [P, cols], dt, offset=at)[:, :]

    def here():
        return off[0]

    XT = place("residual", KC * T).rearrange("p (k t) -> p k t", k=KC)
    XHL = place("x_hi_lo", KC * 2 * T, F32R).rearrange("p (k t) -> p k t", k=KC)
    w_hi = place("w_hi", SLOTS * 2048, F32R).rearrange("p (s k n) -> p s k n", s=SLOTS, k=4)
    raw_at = here()
    w_lo = place("w_lo", SLOTS * 2048, F32R).rearrange("p (s k n) -> p s k n", s=SLOTS, k=4)
    w_raw = place("w_raw", SLOTS * 2048, F32, at=raw_at).rearrange("p (s k n) -> p s k n", s=SLOTS, k=4)
    PAR = place("params", 280)
    NW = place("norm_weights", NORMS * KC)
    GPAR = place("gate_params", 8)
    IO = place("ident_ones", 256)
    IDENT, ONES = IO[:, 0:128], IO[:, 128:256]
    RSTD = place("rstd_rows", T)
    LO = place("lo_ring", 2 * T).rearrange("p (s t) -> p s t", s=2)
    SUM = place("sum_ring", 2 * T).rearrange("p (s t) -> p s t", s=2)
    SMALL = place("small", 128)
    MS2, R2 = SMALL[:, 0:2], SMALL[:, 2:4]
    MHALF = SMALL[:, 4:12]
    SS, RR = SMALL[:, 16:24], SMALL[:, 24:32]
    CO = SMALL[:, 32:48].rearrange("p (c b) -> p c b", c=4)
    MSO, RO = SMALL[:, 48:52], SMALL[:, 52:56]
    MX, NM, SUMP, SE, DEN, REC = (SMALL[:, 56 + 2 * i:58 + 2 * i] for i in range(6))
    EXPA = SMALL[:, 70:71]
    SEL = place("row_selectors", 16, F32R)
    M0 = here()

    def at(name, start, cols, dt=F32):
        assert M0 + (start + cols) * 4 <= 229344, name
        return place(name, cols, dt, at=M0 + start * 4)

    CON = at("consts", 0, CONST_N)
    con = {n: CON[:, CONST_AT[n]:CONST_AT[n] + w] for n, w in CONST.items()}
    m = CONST_N
    qkv = at("gdn_qkv", m, 24 * T)
    QKV = qkv.rearrange("p (c t) -> p c t", c=24)
    STR = at("gate_rows_hi_lo", CONST_AT["reset"], T, F32R)
    QKV3 = qkv.rearrange("p (a c) -> p a c", a=3)
    QKVb = [QKV3[:, i, :] for i in range(3)]
    m += 24 * T
    Z = at("gdn_z", m, 8 * T).rearrange("p (c t) -> p c t", c=8)
    m += 8 * T
    SBX = at("sb_qkv", m, 12 * T).rearrange("p (c t) -> p c t", c=12)
    WAB_N = 64 * (KC + 1)
    WABH, WABL = at("wab_hi", m, WAB_N, F32R), at("wab_lo", m + WAB_N, WAB_N, F32R)
    WABR = at("wab_raw", m + WAB_N, WAB_N)
    m += 12 * T
    SWX = at("swa_qkv", m, 8 * T).rearrange("p (c t) -> p c t", c=8)
    CV = at("conv_in", m, 4 * 260).rearrange("p (s t) -> p s t", s=4)
    CY = at("conv_out", m + 4 * 260, 2 * T).rearrange("p (s t) -> p s t", s=2)
    m += 8 * T
    ST = at("gate_rows", m, T)
    COL = at("gate_cols", m + T, T).rearrange("p (t r) -> p t r", t=2)
    BE = at("beta_eg", m + 2 * T, 16).rearrange("p (t h) -> p t h", t=2)
    DEC = at("chunk_decay", m + 2 * T + 16, 32)
    m += 2 * T + 48
    A0 = m
    SCRATCH = at("scratch", A0, 10 * 512).rearrange("p (a c) -> p a c", a=10)
    A = [SCRATCH[:, i, :] for i in range(10)]
    G = [at(f"gate_tmp{i}", A0 + 2048 + T * i, T) for i in range(8)]
    S_ = [None] + [A[n // 3 + 6][:, 256 * ((n - 1) % 2):256 * ((n - 1) % 2 + 1)] for n in (1, 2, 3)]
    KF, VF = QKVb[1][:, 0:1024], QKVb[2][:, 0:1024]
    SBZ, SBE, SBV = KF[:, 0:384], KF[:, 384:768], KF[:, 768:1024]
    SBL, SBM = VF[:, 0:384], VF[:, 384:768]
    SWS, SWP = KF[:, 0:512], KF[:, 512:1024]
    SWV, SWT = VF[:, 0:512], VF[:, 512:896]
    MID = at("mid_hi_lo", 0, F_PARTS[0] * 2 * T, F32R).rearrange("p (k t) -> p k t", k=F_PARTS[0])
    f = F_PARTS[0] * 2 * T
    GP = at("gate_in", f, 4 * 260).rearrange("p (s t) -> p s t", s=4)
    GY = at("gate_out", f + 4 * 260, 4 * T).rearrange("p (s t) -> p s t", s=4)
    VV = at("value", f + 4 * 260 + 4 * T, 4 * T).rearrange("p (s t) -> p s t", s=4)
    SQ0 = [at(f"first_squares_{j}", CONST_N + 1024 * j, 1024) for j in range(4)]
    XW0 = [at(f"first_x_times_w_{j}", CONST_N + 4096 + 1024 * j, 1024) for j in range(4)]
    f = A0
    SQ = at("squares", f, 1024)
    PART = at("part_sums", f + 1024, 4 * T).rearrange("p (s t) -> p s t", s=4)
    XW = at("x_times_w", f + 2048, 1024)
    DIAG = at("rstd_diag", f + 3072, T)

    PS = nc.alloc_psum_tensor("banks", [P, 8, 512], F32)

    def signal(name, per_layer=0, before=0):
        return Signal(nc.alloc_semaphore(name), per_layer, before)

    x_loaded = [signal(f"x_loaded_{j}") for j in range(4)]
    io_loaded = signal("io_loaded")
    nw_loaded = signal("nw_loaded")
    par_loaded = signal("par_loaded", 16 * 3)
    wab_loaded = signal("wab_loaded", 16)
    whi_ready = signal("whi_ready", 2 * U_LAYER)
    wlo_ready = signal("wlo_ready", 2 * U_LAYER)
    unit_used = signal("unit_used", U_LAYER)
    bank_done = signal("bank_done", E_LAYER // 4 * 3)
    lo_ready = signal("lo_ready", E_LAYER)
    sum_ready = signal("sum_ready", E_LAYER, 4)
    chunk_done = signal("chunk_done", E_LAYER, 2)
    sq_ready = signal("sq_ready", 8)
    part_ready = signal("part_ready", 8)
    xw_ready = signal("xw_ready", 8)
    xhi_ready = signal("xhi_ready", 8)
    xlo_ready = signal("xlo_ready", 8)
    colsum_done = signal("colsum_done", 2)
    ms_ready = signal("ms_ready", 2)
    r_ready = signal("r_ready", 2)
    diag_ready = signal("diag_ready", 2)
    rstd_row_done = signal("rstd_row_done", 2)
    rstd_ready = signal("rstd_ready", 2)
    set_up = signal("set_up")
    pads_ready = signal("pads_ready", 1)
    tap0_ready = signal("tap0_ready", 24)
    tap_done = signal("tap_done", 72)
    silu_done = signal("silu_done", 32)
    gtap0_ready = signal("gtap0_ready", FC)
    gtap_done = signal("gtap_done", 2 * FC)
    gsilu_done = signal("gsilu_done", FC)
    gated_done = signal("gated_done", FC)
    midhi_ready = signal("midhi_ready", FC)
    midlo_ready = signal("midlo_ready", FC)
    wabhi_ready = signal("wabhi_ready", 1)
    wablo_ready = signal("wablo_ready", 1)
    ab_done = signal("ab_done", 1)
    ga = signal("ga", 7)
    gd = signal("gd", 10)
    gate_t_done = signal("gate_t_done", 1)
    dec_done = signal("dec_done", 1)
    gate_cols_ready = signal("gate_cols_ready", 3)
    sel_ready = signal("sel_ready")
    sthi_ready = signal("sthi_ready", 1)
    stlo_ready = signal("stlo_ready", 2)
    nat_done = signal("nat_done", 12)
    sqn_ready = signal("sqn_ready", 8)
    ss_ready = signal("ss_ready", 12)
    rr_ready = signal("rr_ready", 4)
    co_ready = signal("co_ready", 16)
    nat_ready = signal("nat_ready", 24)
    back_done = signal("back_done", 12)
    back_ready = signal("back_ready", 12)
    grow_done = signal("grow_done", 4)
    beta_done = signal("beta_done", 4)
    qk_done = signal("qk_done", 4)
    gm_ready = signal("gm_ready", 4)
    e1_ready = signal("e1_ready", 4)
    qkg_ready = signal("qkg_ready", 4)
    w1_ready = signal("w1_ready", 4)
    at_ready = signal("at_ready", 4)
    bt_ready = signal("bt_ready", 24)
    e0_ready = signal("e0_ready", 4)
    x_done = signal("x_done", 24)
    xs_ready = signal("xs_ready", 20)
    dx_done = signal("dx_done", 16)
    ex_done = signal("ex_done", 20)
    d_ready = signal("d_ready", 20)
    e_ready = signal("e_ready", 20)
    u_done = signal("u_done", 4)
    wdt_done = signal("wdt_done", 4)
    u_ready = signal("u_ready", 4)
    wdt_ready = signal("wdt_ready", 4)
    wd_ready = signal("wd_ready", 4)
    kv_done = signal("kv_done", 4)
    mt_done = signal("mt_done", 4)
    mt_ready = signal("mt_ready", 4)
    mst_done = signal("mst_done", 8)
    ds_ready = signal("ds_ready", 8)
    s_ready = signal("s_ready", 12)
    ws_done = signal("ws_done", 4)
    v_ready = signal("v_ready", 4)
    o_done = signal("o_done", 4)
    os_ready = signal("os_ready", 4)
    osq_ready = signal("osq_ready", 4)
    osum_done = signal("osum_done", 4)
    mso_ready = signal("mso_ready", 4)
    ro_ready = signal("ro_ready", 4)
    odiag_ready = signal("odiag_ready", 4)
    orow_done = signal("orow_done", 4)
    oz_ready = signal("oz_ready", 4)
    gdn_out = signal("gdn_out", 4)
    sb_z_done = signal("sb_z_done", 4)
    sb_zs = signal("sb_zs", 4)
    sb_abs = signal("sb_abs", 4)
    sb_exp = signal("sb_exp", 4)
    sb_ln = signal("sb_ln", 4)
    sb_v = signal("sb_v", 8)
    sb_zm = signal("sb_zm", 4)
    sb_sp = signal("sb_sp", 8)
    sb_c_done = signal("sb_c_done", 4)
    sb_y = signal("sb_y", 4)
    sb_a = signal("sb_a", 4)
    sb_o_done = signal("sb_o_done", 4)
    sb_out = signal("sb_out", 4)
    rot_done = signal("rot_done", 3)
    xcos = signal("xcos", 3)
    xsin = signal("xsin", 3)
    roped = signal("roped", 3)
    sw_vt_done = signal("sw_vt_done", 1)
    sw_v = signal("sw_v", 1)
    sw_s_done = signal("sw_s_done", 4)
    sw_s = signal("sw_s", 12)
    sw_p = signal("sw_p", 12)
    sw_den = signal("sw_den", 12)
    sw_pt_done = signal("sw_pt_done", 4)
    sw_pt = signal("sw_pt", 4)
    sw_o_done = signal("sw_o_done", 4)
    sw_out = signal("sw_out", 4)
    ohi_ready = signal("ohi_ready", 4)
    olo_ready = signal("olo_ready", 4)
    stored = signal("stored")
    fin_y = signal("fin_y")
    fin_xw = signal("fin_xw")
    last_xw = signal("last_xw")

    raw_ready = [nc.alloc_semaphore(f"raw_ready_{s}") for s in range(SLOTS)]


    u_o, e_o = U_IN, E_IN
    u_up = [u_o + U_O, u_o + U_O + U_UP[0] + U_DN[0]]
    u_dn = [u_up[0] + U_UP[0], u_up[1] + U_UP[1]]
    e_up = [e_o + E_O, e_o + E_O + E_UP[0] + E_DN[0]]
    e_dn = [e_up[0] + E_UP[0], e_up[1] + E_UP[1]]

    def conv_group(name):
        return {"q": 0, "k": 8, "v": 16}[name[0]] + 4 * int(name[1]) if name[0] in "qkv" else None

    n_conv = lambda i: sum(IN_ORDER[j][0] in "qkv" for j in range(i))
    n_silu = lambda i: sum(IN_ORDER[j][0] in "qkvz" for j in range(i))

    def blk(t, i):
        return slice((2 * t + i) * P, (2 * t + i + 1) * P)

    def b4(ap):
        return ap.rearrange("p (b c) -> p b c", b=4)

    def pair(ap3, c0):
        return ap3[:, c0:c0 + 2, :].rearrange("p i (t c) -> p t i c", t=2)

    def tb(ap, n=P):
        return ap.unsqueeze(2).to_broadcast([P, 4, n])

    def b22(ap):
        return ap.rearrange("p (t i c) -> p t i c", t=2, i=2)

    def KNT(g):
        return QKVb[1][:, 512 * g:512 * g + 512]

    def QNT(g):
        return QKVb[0][:, 512 * g:512 * g + 512]

    def QET(g):
        return QKVb[2][:, 512 * g:512 * g + 512]

    PAIR = PS[:, 4:6, :].rearrange("p b (q c) -> p (b q) c", q=2)

    block = nc.Block()
    block.__enter__()

    @block.sync
    def _(sp):
        sp.dma_start(NW, norm_w).then_inc(nw_loaded.sem, 16)

        def load(u, s):
            sp.dma_start(w_raw[:, s].rearrange("p k n -> p (k n)"),
                         units[bass.ds(u, 1)].rearrange("a p n -> p (a n)")).then_inc(raw_ready[s], 16)

        for s in range(SLOTS):
            sp.dma_start(XT[:, 4 * s:4 * s + 4, :], x_in[:, 4 * s:4 * s + 4, :]).then_inc(x_loaded[s].sem, 16)
            if s == 1:
                sp.dma_start(IO, ident_ones).then_inc(io_loaded.sem, 16)
            if s < AHEAD:
                load(s, s)
        for s in range(AHEAD, SLOTS):
            load(s, s)
        with sp.Fori(1, (U_ALL + SLOTS) // SLOTS) as i:
            for s in range(SLOTS):
                sp.wait_ge(unit_used.sem, i * SLOTS + (s - SLOTS + 1))
                load(i * SLOTS + s, s)
        for j in range(4):
            sp.wait_ge(fin_y.sem, j + 1)
            sp.dma_start(out[:, 4 * j:4 * j + 4, :], XT[:, 4 * j:4 * j + 4, :]).then_inc(stored.sem, 16)
        sp.wait_ge(stored.sem, 64)

    @block.tensor
    def _(pe):
        mm, tr = nc.tensor.matmul, nc.tensor.transpose

        def colsum(l, n):
            for j in range(4):
                pe.wait_ge(part_ready.sem, part_ready.of(l, 4 * n + j + 1))
                for t in range(2):
                    r = mm(PS[:, 4 + t, 0:1], PART[:, j, t * P:(t + 1) * P], ONES[:, 0:1],
                           start=(j == 0), stop=(j == 3))
            r.then_inc(colsum_done.sem, 1)

        def rows(done):
            mm(PS[:, 5, 0:T], ONES, DIAG, start=True, stop=True).then_inc(done, 1)

        def layer(l):

            def gemm(u, e, n_units, slot0, rhs, ready=None, after=None, weave=None):
                for j in range(n_units):
                    pe.wait_ge(wlo_ready.sem, wlo_ready.of(l, (u + (j + 1)) * 2))
                    if ready:
                        ready(j)
                    s = (slot0 + j) % SLOTS
                    for n in range(4):
                        if j == 0:
                            pe.wait_ge(sum_ready.sem, sum_ready.of(l, e + (n + 1 - 4)))
                        cols = slice(n * P, (n + 1) * P)
                        for k in range(4):
                            x = rhs(4 * j + k)
                            last = j == n_units - 1 and k == 3
                            mm(PS[:, n, :], w_hi[:, s, k, cols], x, start=(j == 0 and k == 0), stop=False)
                            r = mm(PS[:, n, T:2 * T], w_lo[:, s, k, cols], x[:, 0:T], start=False, stop=last)
                            if k == 3 and n == 3:
                                r.then_inc(unit_used.sem, 1)
                            elif last:
                                r.then_inc(bank_done.sem, 1)
                        if weave:
                            weave()
                    if after:
                        after(j)

            def gates_strand():
                pe.wait_ge(wablo_ready.sem, wablo_ready.of(l, 1))
                for k in range(KC):
                    c = slice(64 * k, 64 * k + P)
                    mm(PS[:, 4, :], WABH[:, c], XHL[:, k, :], start=(k == 0), stop=False)
                    r = mm(PS[:, 4, T:2 * T], WABL[:, c], XHL[:, k, 0:T], start=False, stop=(k == KC - 1))
                r.then_inc(ab_done.sem, 1)
                yield from beats(12)
                pe.wait_ge(gd.sem, gd.of(l, 10))
                pe.wait_ge(ga.sem, ga.of(l, 7))
                for t in range(2):
                    r = tr(PS[:, 6, t * P:(t + 1) * P], ST[:, t * P:(t + 1) * P], IDENT)
                r.then_inc(gate_t_done.sem, 1)
                for h in range(GH):
                    r = mm(PS[:, 7, 4 * h:4 * h + 4], IDENT[64:72, 64 + h:65 + h].to_broadcast([8, P]),
                           ST[64:72, CH - 1:T:CH], start=True, stop=True)
                r.then_inc(dec_done.sem, 1)
                yield

            def gdn_strand():
                yield from beats(GDN_START)
                pe.wait_ge(gate_cols_ready.sem, gate_cols_ready.of(l, 3))
                for g in range(4):
                    yield from gdn(g)

            def gdn(g):
                hh = 2 * g
                pe.wait_ge(silu_done.sem, silu_done.of(l, 4 * n_silu(2 if g < 2 else 6)))
                if g:
                    pe.wait_ge(gdn_out.sem, gdn_out.of(l, g))
                for b, c in ((4, 8), (5, 0), (6, 16)):
                    if b == 6:
                        yield from beats(GDN_BEATS["keys"])
                        pe.wait_ge(silu_done.sem, silu_done.of(l, 4 * n_silu(3 if g < 2 else 7)))
                    for t in range(2):
                        for i in range(2):
                            r = tr(PS[:, b, blk(t, i)], QKV[:, c + hh + i, t * P:(t + 1) * P], IDENT)
                    r.then_inc(nat_done.sem, 1)
                yield from beats(GDN_BEATS["values"])
                for b, a, n in ((4, 3, 3), (5, 4, 5), (6, 5, 6)):
                    pe.wait_ge(nat_ready.sem, nat_ready.of(l, 6 * g + n))
                    for q in range(4):
                        r = tr(PS[:, b, q * P:(q + 1) * P], A[a][:, q * P:(q + 1) * P], IDENT)
                    r.then_inc(back_done.sem, 1)
                yield from beats(GDN_BEATS["back"])
                pe.wait_ge(back_ready.sem, back_ready.of(l, 3 * g + 3))
                if g == 0:
                    pe.wait_ge(stlo_ready.sem, stlo_ready.of(l, 2))
                for i in range(2):
                    r = mm(b22(PS[:, 6, :])[:, :, i, :], SEL[:, hh + i:hh + i + 1].to_broadcast([P, P]),
                           STR.rearrange("p (t c) -> p t c", t=2), start=True, stop=True)
                r.then_inc(grow_done.sem, 1)
                for q in range(4):
                    c = slice(512 * g + q * P, 512 * g + (q + 1) * P)
                    r = mm(PAIR[:, q, :].rearrange("p (a c) -> p a c", a=2), QKV3[:, 1, c], QKV3[:, 0:2, c],
                           start=True, stop=True)
                r.then_inc(qk_done.sem, 1)
                yield from beats(GDN_BEATS["products"])
                pe.wait_ge(gm_ready.sem, gm_ready.of(l, g + 1))
                for i in range(2):
                    r = mm(b22(PS[:, 6, :])[:, :, i, :], SEL[:, 8 + hh + i:9 + hh + i].to_broadcast([P, P]),
                           STR.rearrange("p (t c) -> p t c", t=2), start=True, stop=True)
                r.then_inc(beta_done.sem, 1)
                yield from beats(GDN_BEATS["beta"])
                pe.wait_ge(bt_ready.sem, bt_ready.of(l, 6 * g + 1))
                for q in range(4):
                    c = slice(q * P, (q + 1) * P)
                    r = tr(PS[:, 4, c], A[8][:, c], IDENT)
                r.then_inc(x_done.sem, 1)
                yield from beats(GDN_BEATS["transpose"])
                for j in range(1, 6):
                    bt = A[8] if j % 2 == 0 else A[6]
                    pe.wait_ge(bt_ready.sem, bt_ready.of(l, 6 * g + j + 1))
                    pe.wait_ge(d_ready.sem, d_ready.of(l, 5 * g + j))
                    for q in range(4):
                        c = slice(q * P, (q + 1) * P)
                        r = mm(PS[:, 5, c], bt[:, c], A[4][:, c], start=True, stop=True)
                    r.then_inc(x_done.sem, 1)
                    yield from beats(GDN_BEATS["x"])
                    pe.wait_ge(xs_ready.sem, xs_ready.of(l, 5 * g + j))
                    if j > 1:
                        pe.wait_ge(e_ready.sem, e_ready.of(l, 5 * g + j - 1))
                    else:
                        pe.wait_ge(e0_ready.sem, e0_ready.of(l, g + 1))
                    if j < 5:
                        for q in range(4):
                            c = slice(q * P, (q + 1) * P)
                            r = mm(PS[:, 4, c], A[5][:, c], A[7][:, c], start=True, stop=True)
                        r.then_inc(dx_done.sem, 1)
                    for q in range(4):
                        c = slice(q * P, (q + 1) * P)
                        r = mm(PS[:, 6, c], A[7][:, c], A[5][:, c], start=True, stop=True)
                    r.then_inc(ex_done.sem, 1)
                    yield from beats(GDN_BEATS["e"])
                pe.wait_ge(e_ready.sem, e_ready.of(l, 5 * g + 5))
                for q in range(4):
                    c = slice(q * P, (q + 1) * P)
                    r = mm(PAIR[:, q, :].rearrange("p (a c) -> p a c", a=2), A[5][:, c], SCRATCH[:, 0:3:2, c],
                           start=True, stop=True)
                r.then_inc(u_done.sem, 1)
                for q in range(4):
                    c = slice(q * P, (q + 1) * P)
                    r = mm(PS[:, 6, c], A[0][:, c], A[5][:, c], start=True, stop=True)
                r.then_inc(wdt_done.sem, 1)
                yield from beats(GDN_BEATS["u"])
                pe.wait_ge(u_ready.sem, u_ready.of(l, g + 1))
                pe.wait_ge(wd_ready.sem, wd_ready.of(l, g + 1))
                for n, bank, half in ((0, 4, 0), (2, 4, 1), (1, 5, 0)):
                    t, r0 = n // 2, CH * (n % 2)
                    for i in range(2):
                        r = mm(PS[:, bank, blk(half, i)], A[1][r0:r0 + CH, blk(t, i)], A[2][r0:r0 + CH, blk(t, i)],
                               start=True, stop=True)
                r.then_inc(kv_done.sem, 1)
                pe.wait_ge(wdt_ready.sem, wdt_ready.of(l, g + 1))
                for n, bank, half in ((1, 5, 1), (2, 6, 0)):
                    t, r0 = n // 2, CH * (n % 2)
                    for i in range(2):
                        r = mm(PS[:, bank, blk(half, i)], A[4][r0:r0 + CH, blk(t, i)], A[1][r0:r0 + CH, blk(t, i)],
                               start=True, stop=True)
                r.then_inc(mt_done.sem, 1)
                yield from beats(GDN_BEATS["kv"])
                pe.wait_ge(mt_ready.sem, mt_ready.of(l, g + 1))
                for n in (1, 2):
                    pe.wait_ge(s_ready.sem, s_ready.of(l, 3 * g + n))
                    for i in range(2):
                        r = mm(PS[:, 6, i * P:(i + 1) * P], A[8][:, blk(n - 1, i)], S_[n][:, i * P:(i + 1) * P],
                               start=True, stop=True)
                    r.then_inc(mst_done.sem, 1)
                    yield from beats(GDN_BEATS["state"])
                pe.wait_ge(s_ready.sem, s_ready.of(l, 3 * g + 3))
                for n in (1, 2, 3):
                    t, r0 = n // 2, CH * (n % 2)
                    for i in range(2):
                        c = slice(blk(t, i).start + r0, blk(t, i).start + r0 + CH)
                        r = mm(PS[r0:r0 + CH, 4, blk(t, i)], A[3][:, c], S_[n][:, i * P:(i + 1) * P],
                               start=True, stop=True)
                r.then_inc(ws_done.sem, 1)
                yield from beats(GDN_BEATS["ws"])
                pe.wait_ge(v_ready.sem, v_ready.of(l, g + 1))
                for t in range(2):
                    for i in range(2):
                        mm(PS[:, 5, blk(t, i)], A[2][:, blk(t, i)], A[9][:, blk(t, i)], start=True, stop=False)
                        for half in range(2):
                            n = 2 * t + half
                            if n:
                                c = slice(blk(t, i).start + CH * half, blk(t, i).start + CH * (half + 1))
                                r = mm(PS[:, 5, c], S_[n][:, i * P:(i + 1) * P], QET(g)[:, c],
                                       start=False, stop=(half == 1))
                r.then_inc(o_done.sem, 1)
                yield from beats(GDN_BEATS["out"])
                pe.wait_ge(osq_ready.sem, osq_ready.of(l, g + 1))
                for q in range(4):
                    r = mm(PS[:, 6, q:q + 1], A[3][:, q * P:(q + 1) * P], ONES[:, 0:1], start=True, stop=True)
                r.then_inc(osum_done.sem, 1)
                yield from beats(GDN_BEATS["sums"])
                pe.wait_ge(odiag_ready.sem, odiag_ready.of(l, g + 1))
                mm(PS[:, 4, :], ONES, A[4], start=True, stop=True).then_inc(orow_done.sem, 1)
                yield from beats(GDN_BEATS["rows"])

            def sb_strand():
                yield from beats(4)
                pe.wait_ge(chunk_done.sem, chunk_done.of(l, 40))
                pe.wait_ge(gdn_out.sem, gdn_out.of(l, 2))
                for h in range(SH):
                    q, k, v = SBX[:, h, :], SBX[:, 4 + h, :], SBX[:, 8 + h, :]
                    if h:
                        pe.wait_ge(sb_out.sem, sb_out.of(l, h))
                    mm(PS[:, 7, 0:256], k[:, 0:P], q, start=True, stop=True)
                    mm(PS[:, 7, 256:384], k[:, P:T], q[:, P:T], start=True, stop=True)
                    tr(PS[:, 7, 384:512], v[:, 0:P], IDENT).then_inc(sb_z_done.sem, 1)
                    yield from beats(SB_BEATS[0])
                    pe.wait_ge(sb_sp.sem, sb_sp.of(l, 2 * h + 2))
                    pe.wait_ge(sb_v.sem, sb_v.of(l, 2 * h + 1))
                    mm(PS[:, 7, 0:256], con["negu"], SBL[:, 0:256], start=True, stop=False)
                    mm(PS[:, 7, 128:256], con["negone"], SBL[:, 256:384], start=False, stop=True)
                    mm(PS[:, 7, 256:384], con["negu"], SBL[:, 256:384], start=True, stop=True)
                    tr(PS[:, 7, 384:512], v[:, P:T], IDENT).then_inc(sb_c_done.sem, 1)
                    yield from beats(SB_BEATS[1])
                    pe.wait_ge(sb_a.sem, sb_a.of(l, h + 1))
                    pe.wait_ge(sb_v.sem, sb_v.of(l, 2 * h + 2))
                    mm(PS[:, 7, 0:256], SBV[:, 0:P], SBE[:, 0:256], start=True, stop=False)
                    mm(PS[:, 7, 128:256], SBV[:, P:T], SBE[:, 256:384], start=False, stop=True).then_inc(
                        sb_o_done.sem, 1)
                    yield from beats(SB_BEATS[2])

            def sw_strand():
                yield from beats(8)
                pe.wait_ge(sb_out.sem, sb_out.of(l, 4))
                for c in range(3):
                    pe.wait_ge(chunk_done.sem, chunk_done.of(l, 48 if c < 2 else 52))
                    if c:
                        pe.wait_ge(xsin.sem, xsin.of(l, c))
                    mm(PS[:, 7, :], con["rot"], SWX[:, 2 * c:2 * c + 2, :].rearrange("p a t -> p (a t)"),
                       start=True, stop=True).then_inc(rot_done.sem, 1)
                    yield from beats((3, 6, 1)[c])
                pe.wait_ge(xsin.sem, xsin.of(l, 3))
                for v in range(2):
                    for t in range(2):
                        r = tr(PS[:, 7, blk(v, t)], SWX[:, 6 + v, t * P:(t + 1) * P], IDENT)
                r.then_inc(sw_vt_done.sem, 1)
                yield
                pe.wait_ge(roped.sem, roped.of(l, 3))
                pe.wait_ge(sw_v.sem, sw_v.of(l, 1))
                for h in range(WH_):
                    v = h // (WH_ // KVH)
                    if h:
                        pe.wait_ge(sw_out.sem, sw_out.of(l, h))
                    for t in range(2):
                        r = mm(PS[:, 7, t * T:(t + 1) * T], SWX[:, h, t * P:(t + 1) * P], SWX[:, 4 + v, :],
                               start=True, stop=True)
                    r.then_inc(sw_s_done.sem, 1)
                    yield from beats(SW_BEATS[0])
                    pe.wait_ge(sw_den.sem, sw_den.of(l, 3 * h + 3))
                    tr(PS[:, 7, 0:P], SWP[:, 0:P], IDENT)
                    tr(PS[:, 7, P:2 * P], SWP[:, T:T + P], IDENT)
                    tr(PS[:, 7, 2 * P:3 * P], SWP[:, T + P:2 * T], IDENT).then_inc(sw_pt_done.sem, 1)
                    yield from beats(SW_BEATS[1])
                    pe.wait_ge(sw_pt.sem, sw_pt.of(l, h + 1))
                    mm(PS[:, 7, 0:T], SWV[:, blk(v, 0)], SWT[:, 0:T], start=True, stop=False)
                    mm(PS[:, 7, P:T], SWV[:, blk(v, 1)], SWT[:, T:T + P], start=False, stop=True).then_inc(
                        sw_o_done.sem, 1)
                    yield from beats(SW_BEATS[2])

            def norm(n, j):
                if j == 1:
                    colsum(l, n)
                elif j == 2:
                    pe.wait_ge(diag_ready.sem, diag_ready.of(l, n + 1))
                    rows(rstd_row_done.sem)

            x_rows = lambda k: XHL[:, k, :]
            strands = Strands()
            for i in range(IN_TILES):
                if i == GATES_FROM:
                    strands.begin(gates_strand())
                if i == GDN_FROM:
                    strands.begin(gdn_strand())
                if i == SB_FROM:
                    strands.begin(sb_strand())
                if i == SW_FROM:
                    strands.begin(sw_strand())
                gemm(4 * i, 4 * i, 4, 0, x_rows, ready=(lambda j: pe.wait_ge(xlo_ready.sem, xlo_ready.of(l, j + 1))) if i == 0 else None,
                     after=(lambda j: norm(0, j)) if i == 0 else None, weave=strands.beat)
            for half in range(2):
                for i in range(4):
                    n = 4 * half + i
                    gemm(u_o + 2 * n, e_o + 4 * n, 2, 2 * n, lambda k, half=half: XHL[:, 8 * half + k, :],
                         ready=lambda j, half=half: pe.wait_ge(olo_ready.sem, olo_ready.of(l, 2 * half + j + 1)), weave=strands.beat)
                strands.finish()
            for part in range(2):
                if part == 0:
                    gemm(u_up[0], e_up[0], 4, 0, x_rows, ready=lambda j: pe.wait_ge(xlo_ready.sem, xlo_ready.of(l, 4 + j + 1)),
                         after=lambda j: norm(1, j))
                    gemm(u_up[0] + 4, e_up[0] + 4, 4, 0, x_rows)
                with pe.Fori(1 - part, F_PARTS[part] // 4) as i:
                    for j in range(2):
                        gemm(i * 8 + (u_up[part] + 4 * j), i * 8 + (e_up[part] + 4 * j), 4, 0, x_rows)
                n_units = F_PARTS[part] // 4
                f0 = sum(F_PARTS[:part])
                mid = lambda k: MID[:, k, :]

                def mid_ready(j, f0=f0):
                    pe.wait_ge(midlo_ready.sem, midlo_ready.of(l, f0 + 4 * j + 4))
                if part == 0:
                    with pe.Fori(0, 2) as i:
                        for j in range(2):
                            gemm(i * (2 * n_units) + (u_dn[0] + j * n_units), i * 8 + (e_dn[0] + 4 * j), n_units,
                                 j * n_units, mid, ready=mid_ready)
                else:
                    for j in range(4):
                        gemm(u_dn[1] + j * n_units, e_dn[1] + 4 * j, n_units, j * n_units, mid, ready=mid_ready)

        pe.wait_ge(io_loaded.sem, 16)
        with pe.Fori(0, DEPTH) as l:
            layer(l)
        colsum(DEPTH, 0)
        pe.wait_ge(diag_ready.sem, diag_ready.of(DEPTH, 1))
        rows(rstd_row_done.sem)

    @block.scalar
    def _(act):
        A_ = nc.scalar.activation

        def first_hi(j):
            act.wait_ge(xw_ready.sem, xw_ready.of(0, j + 1))
            A_(XHL[:, 4 * j:4 * j + 4, 0:T], XW0[j].rearrange("p (k t) -> p k t", k=4), ACT.Copy).then_inc(
                xhi_ready.sem, 1)

        def first_squares(j):
            act.wait_ge(x_loaded[j].sem, 16)
            A_(SQ0[j], XT[:, 4 * j:4 * j + 4, :].rearrange("p k t -> p (k t)"), ACT.Square).then_inc(
                sq_ready.sem, 1)

        def norm_tile(l, n, j):
            x4 = XT[:, 4 * j:4 * j + 4, :].rearrange("p k t -> p (k t)")
            if n == 1:
                act.wait_ge(chunk_done.sem, chunk_done.of(l, E_IN + 16 + 4 * j + 4))
            else:
                act.wait_ge(chunk_done.sem, chunk_done.of(l, E_LAYER - 16 + 4 * j + 4))
            act.wait_ge(part_ready.sem, part_ready.of(l, 4 * n + j))
            A_(SQ, x4, ACT.Square).then_inc(sq_ready.sem, 1)
            act.wait_ge(xw_ready.sem, xw_ready.of(l, 4 * n + j + 1))
            if n == 1:
                act.wait_ge(unit_used.sem, unit_used.of(l, U_IN + (7, 8, 15, 16)[j]))
            elif n == 2 and j == 0:
                act.wait_ge(unit_used.sem, unit_used.of(l, u_dn[1]))
            A_(XHL[:, 4 * j:4 * j + 4, 0:T], XW.rearrange("p (k t) -> p k t", k=4), ACT.Copy).then_inc(
                xhi_ready.sem, 1)

        def rstd(l, n):
            act.wait_ge(rstd_row_done.sem, rstd_row_done.of(l, n + 1))
            A_(RSTD, PS[:, 5, 0:T], ACT.Copy).then_inc(rstd_ready.sem, 1)

        def split(turn, s, h=0):
            act.wait_ge(raw_ready[s], turn * 16 + 16)
            A_(w_hi[:, s, 2 * h:2 * h + 2].rearrange("p k n -> p (k n)"),
               w_raw[:, s, 2 * h:2 * h + 2].rearrange("p k n -> p (k n)"), ACT.Copy).then_inc(whi_ready.sem, 1)

        def split_all(turn, s):
            act.wait_ge(raw_ready[s], turn * 16 + 16)
            A_(w_hi[:, s].rearrange("p k n -> p (k n)"), w_raw[:, s].rearrange("p k n -> p (k n)"),
               ACT.Copy).then_inc(whi_ready.sem, 2)

        act.wait_ge(set_up.sem, 1)
        for j in range(AHEAD):
            first_hi(j)
            for h in range(2):
                split(0, j, h)
        first_hi(2)
        first_squares(0)
        first_squares(1)
        first_hi(3)
        first_squares(2)
        first_squares(3)

        def layer(l):

            def splits(u, n, i=0, step=0):
                for j in range(n):
                    v = u + AHEAD + j
                    split_all(l * (U_LAYER // SLOTS) + (i * (step // SLOTS) + v // SLOTS), v % SLOTS)

            def woven_splits(u, n, before=None):
                for j in range(n):
                    if before:
                        before(j)
                    v = u + AHEAD + j
                    for h in range(2):
                        split(l * (U_LAYER // SLOTS) + v // SLOTS, v % SLOTS, h)
                        if j < n - 1:
                            strands.beats(2)

            def lo(e, e4, n, u_last):
                if n < 3:
                    act.wait_ge(bank_done.sem, bank_done.of(l, e4 + (n + 1)))
                else:
                    act.wait_ge(unit_used.sem, unit_used.of(l, u_last))
                act.wait_ge(sum_ready.sem, sum_ready.of(l, e + (n + 1 - 2)))
                A_(LO[:, n % 2, :], PS[:, n, T:2 * T], ACT.Copy).then_inc(lo_ready.sem, 1)

            def tile_lo(u, e, e4, n_units, between=None):
                for n in range(4):
                    lo(e, e4, n, u + n_units)
                    strands.beat()
                    if between:
                        between(n)

            def wab_hi():
                act.wait_ge(wab_loaded.sem, wab_loaded.of(l, 16))
                A_(WABH, WABR, ACT.Copy).then_inc(wabhi_ready.sem, 1)

            def in_tile(i):
                def before(j):
                    if i == 0 and j == 3:
                        rstd(l, 0)
                        wab_hi()
                    elif i == IN_TILES - 1 and j in (1, 2):
                        o_hi(j - 1)
                woven_splits(4 * i, 4, before)
                if i == 0:
                    act.wait_ge(par_loaded.sem, par_loaded.of(l, 48))
                e, group, z = 4 * i, conv_group(IN_ORDER[i]), IN_ORDER[i][0] == "z"
                c0, s0 = 4 * n_conv(i), 4 * n_silu(i)

                def tap0(n):
                    act.wait_ge(chunk_done.sem, chunk_done.of(l, e + n + 1))
                    if n >= 2:
                        act.wait_ge(silu_done.sem, silu_done.of(l, s0 + n - 1))
                    A_(CY[:, n % 2, :], CV[:, n, 3:3 + T], ACT.Copy,
                       scale=PAR[:, PAR_GC + 3 * 24 + group + n:PAR_GC + 3 * 24 + group + n + 1]).then_inc(
                           tap0_ready.sem, 1)

                def silu(n):
                    act.wait_ge(tap_done.sem, tap_done.of(l, 3 * (c0 + n) + 3))
                    A_(QKV[:, group + n, :], CY[:, n % 2, :], ACT.Silu).then_inc(silu_done.sem, 1)

                def silu_z(n):
                    act.wait_ge(chunk_done.sem, chunk_done.of(l, e + n + 1))
                    zc = Z[:, 4 * int(IN_ORDER[i][1]) + n, :]
                    A_(zc, zc, ACT.Silu).then_inc(silu_done.sem, 1)

                def conv_strand():
                    tap0(0)
                    tap0(1)
                    yield from beats(2)
                    silu(0)
                    tap0(2)
                    yield from beats(2)
                    silu(1)
                    tap0(3)
                    yield from beats(2)
                    silu(2)
                    yield from beats(2)
                    silu(3)

                tile_lo(4 * i, e, 3 * i, 4, (lambda n: silu_z(n - 1) if n else None) if z else None)
                if group is not None:
                    strands.begin(conv_strand())
                elif z:
                    silu_z(3)

            def gates_strand():
                yield
                act.wait_ge(ab_done.sem, ab_done.of(l, 1))
                A_(G[0][0:64, :], PS[0:64, 4, T:2 * T], ACT.Copy).then_inc(ga.sem, 1)
                yield from beats(2)
                act.wait_ge(gd.sem, gd.of(l, 3))
                A_(G[3][0:8, :], G[2][0:8, :], ACT.Abs, bias=GPAR[0:8, 1:2]).then_inc(ga.sem, 1)
                A_(G[4][32:40, :], G[2][32:40, :], ACT.Exp, scale=-1.0).then_inc(ga.sem, 1)
                act.wait_ge(ga.sem, ga.of(l, 2))
                A_(G[3][0:8, :], G[3][0:8, :], ACT.Exp, scale=-1.0).then_inc(ga.sem, 1)
                A_(EXPA[0:8, :], GPAR[0:8, 0:1], ACT.Exp)
                act.wait_ge(ga.sem, ga.of(l, 4))
                A_(G[3][0:8, :], G[3][0:8, :], ACT.Ln, bias=1.0).then_inc(ga.sem, 1)
                yield from beats(4)
                act.wait_ge(gd.sem, gd.of(l, 8))
                A_(ST[64:72, :], G[6][0:8, :], ACT.Exp).then_inc(ga.sem, 1)
                act.wait_ge(gd.sem, gd.of(l, 9))
                A_(ST[96:104, :], G[7][0:8, :], ACT.Exp).then_inc(ga.sem, 1)
                act.wait_ge(gd.sem, gd.of(l, 10))
                act.wait_ge(ga.sem, ga.of(l, 7))
                A_(STR, ST, ACT.Copy).then_inc(sthi_ready.sem, 1)

            def gdn_strand():
                yield from beats(GDN_START)
                for g in range(4):
                    yield from gdn(g)

            def gdn(g):
                for n, (b, a) in enumerate(((4, 6), (5, 7))):
                    act.wait_ge(nat_done.sem, nat_done.of(l, 3 * g + n + 1))
                    if g and n == 0:
                        act.wait_ge(gdn_out.sem, gdn_out.of(l, g))
                    A_(A[a], PS[:, b, :], ACT.Square).then_inc(sqn_ready.sem, 1)
                yield from beats(GDN_BEATS["keys"] + GDN_BEATS["values"])
                for n, (b, dst) in enumerate(((4, KNT(g)), (5, QNT(g)), (6, QET(g)))):
                    act.wait_ge(back_done.sem, back_done.of(l, 3 * g + n + 1))
                    A_(dst, PS[:, b, :], ACT.Copy).then_inc(back_ready.sem, 1)
                yield from beats(GDN_BEATS["back"])
                act.wait_ge(gm_ready.sem, gm_ready.of(l, g + 1))
                A_(A[7], A[6], ACT.Exp, scale=-1.0).then_inc(e1_ready.sem, 1)
                yield from beats(GDN_BEATS["products"])
                yield from beats(GDN_BEATS["beta"] + GDN_BEATS["transpose"])
                for j in range(1, 6):
                    act.wait_ge(x_done.sem, x_done.of(l, 6 * g + j + 1))
                    if j == 1:
                        act.wait_ge(w1_ready.sem, w1_ready.of(l, g + 1))
                        act.wait_ge(qkg_ready.sem, qkg_ready.of(l, g + 1))
                    A_(A[7], PS[:, 5, :], ACT.Copy).then_inc(xs_ready.sem, 1)
                    yield from beats(GDN_BEATS["x"] + GDN_BEATS["e"])
                act.wait_ge(u_done.sem, u_done.of(l, g + 1))
                A_(b4(A[2]), PAIR[:, :, P:2 * P], ACT.Copy).then_inc(u_ready.sem, 1)
                A_(b4(A[4]), PAIR[:, :, 0:P], ACT.Copy).then_inc(wd_ready.sem, 1)
                act.wait_ge(wdt_done.sem, wdt_done.of(l, g + 1))
                A_(A[3], PS[:, 6, :], ACT.Copy).then_inc(wdt_ready.sem, 1)
                yield from beats(GDN_BEATS["u"])
                act.wait_ge(mt_done.sem, mt_done.of(l, g + 1))
                A_(A[8][:, 0:T], PS[:, 5, T:2 * T], ACT.Copy)
                A_(A[8][:, T:2 * T], PS[:, 6, 0:T], ACT.Copy).then_inc(mt_ready.sem, 1)
                yield from beats(GDN_BEATS["kv"] + 2 * GDN_BEATS["state"] + GDN_BEATS["ws"])
                act.wait_ge(o_done.sem, o_done.of(l, g + 1))
                A_(A[3], PS[:, 5, :], ACT.Square).then_inc(osq_ready.sem, 1)
                A_(A[5], PS[:, 5, :], ACT.Copy, scale=PAR[:, PAR_GN:PAR_GN + 1]).then_inc(os_ready.sem, 1)
                yield from beats(GDN_BEATS["out"] + GDN_BEATS["sums"] + GDN_BEATS["rows"])

            def sb_strand():
                yield from beats(4)
                for h in range(SH):
                    act.wait_ge(sb_z_done.sem, sb_z_done.of(l, h + 1))
                    A_(SBZ, PS[:, 7, 0:384], ACT.Copy, scale=SCALE).then_inc(sb_zs.sem, 1)
                    A_(SBV[:, 0:P], PS[:, 7, 384:512], ACT.Copy).then_inc(sb_v.sem, 1)
                    act.wait_ge(sb_zs.sem, sb_zs.of(l, h + 1))
                    A_(SBE, SBZ, ACT.Abs).then_inc(sb_abs.sem, 1)
                    act.wait_ge(sb_abs.sem, sb_abs.of(l, h + 1))
                    A_(SBE, SBE, ACT.Exp, scale=-1.0).then_inc(sb_exp.sem, 1)
                    act.wait_ge(sb_exp.sem, sb_exp.of(l, h + 1))
                    A_(SBL, SBE, ACT.Ln, bias=1.0).then_inc(sb_ln.sem, 1)
                    yield from beats(SB_BEATS[0])
                    act.wait_ge(sb_y.sem, sb_y.of(l, h + 1))
                    A_(SBE, SBM, ACT.Exp).then_inc(sb_a.sem, 1)
                    A_(SBV[:, P:T], PS[:, 7, 384:512], ACT.Copy).then_inc(sb_v.sem, 1)
                    yield from beats(SB_BEATS[1])
                    act.wait_ge(sb_o_done.sem, sb_o_done.of(l, h + 1))
                    A_(SBX[:, h, :], PS[:, 7, 0:T], ACT.Copy).then_inc(sb_out.sem, 1)
                    yield from beats(SB_BEATS[2])

            def sw_strand():
                yield from beats(8 + 3 + 6 + 1)
                act.wait_ge(sw_vt_done.sem, sw_vt_done.of(l, 1))
                A_(SWV, PS[:, 7, :], ACT.Copy).then_inc(sw_v.sem, 1)
                yield
                for h in range(WH_):
                    act.wait_ge(sw_s.sem, sw_s.of(l, 3 * h + 3))
                    for t in range(2):
                        A_(SWP[:, t * T:(t + 1) * T], SWS[:, t * T:(t + 1) * T], ACT.Exp, bias=NM[:, t:t + 1],
                           accum_out=SUMP[:, t:t + 1]).then_inc(sw_p.sem, 1)
                    A_(SE, NM, ACT.Exp, bias=PAR[:, PAR_SK + h:PAR_SK + h + 1]).then_inc(sw_p.sem, 1)
                    yield from beats(SW_BEATS[0])
                    act.wait_ge(sw_pt_done.sem, sw_pt_done.of(l, h + 1))
                    A_(SWT, PS[:, 7, 0:384], ACT.Copy).then_inc(sw_pt.sem, 1)
                    yield from beats(SW_BEATS[1])
                    act.wait_ge(sw_o_done.sem, sw_o_done.of(l, h + 1))
                    A_(SWX[:, h, :], PS[:, 7, 0:T], ACT.Copy).then_inc(sw_out.sem, 1)
                    yield from beats(SW_BEATS[2])

            def o_hi(kg):
                src = (QKV[:, 0:4, :], SBX[:, 0:4, :], QKV[:, 4:8, :], SWX[:, 0:4, :])[kg]
                act.wait_ge(unit_used.sem, unit_used.of(l, U_IN - 3 + kg))
                if kg == 0:
                    act.wait_ge(gdn_out.sem, gdn_out.of(l, 2))
                elif kg == 1:
                    act.wait_ge(sb_out.sem, sb_out.of(l, 4))
                elif kg == 2:
                    act.wait_ge(gdn_out.sem, gdn_out.of(l, 4))
                else:
                    act.wait_ge(sw_out.sem, sw_out.of(l, 4))
                A_(XHL[:, 4 * kg:4 * kg + 4, 0:T], src, ACT.Copy).then_inc(ohi_ready.sem, 1)

            def up_pair(i, part, first=False):
                u, e, e4 = i * 8 + u_up[part], i * 8 + e_up[part], i * 6 + e_up[part] // 4 * 3
                f0 = sum(F_PARTS[:part])
                fc = i * 4 + f0
                if first:
                    splits(u_up[part], 3)
                    rstd(l, 1)
                    splits(u_up[part] + 3, 1)
                else:
                    splits(u_up[part], 4, i, 8)

                def tap0(n):
                    act.wait_ge(chunk_done.sem, chunk_done.of(l, e + (n + 1)))
                    A_(GY[:, n, :], GP[:, n, 2:2 + T], ACT.Identity,
                       scale=PAR[:, bass.ds(fc + (PAR_FCW + 2 * FC + n), 1)],
                       bias=PAR[:, bass.ds(fc + (PAR_FB + n), 1)]).then_inc(gtap0_ready.sem, 1)

                def silu(n):
                    act.wait_ge(gtap_done.sem, gtap_done.of(l, fc * 2 + (2 * n + 2)))
                    A_(GY[:, n, :], GY[:, n, :], ACT.Silu).then_inc(gsilu_done.sem, 1)

                def between(n):
                    if n:
                        tap0(n - 1)
                    if n == 3:
                        silu(0)
                tile_lo(u, e, e4, 4, between)
                tap0(3)
                splits(u_up[part] + 4, 1, i, 8)
                for n in (1, 2, 3):
                    silu(n)
                splits(u_up[part] + 5, 3, i, 8)

                def hi(n):
                    act.wait_ge(gated_done.sem, gated_done.of(l, fc + (n + 1)))
                    A_(MID[:, bass.ds(i * 4 + n, 1), 0:T], VV[:, n:n + 1, :], ACT.Copy).then_inc(
                        midhi_ready.sem, 1)

                tile_lo(u + 4, e + 4, e4 + 3, 4, lambda n: hi(n - 2) if n >= 2 else None)
                hi(2)
                hi(3)

            strands = Strands()
            for i in range(IN_TILES):
                if i == GATES_FROM:
                    strands.begin(gates_strand())
                if i == GDN_FROM:
                    strands.begin(gdn_strand())
                if i == SB_FROM:
                    strands.begin(sb_strand())
                if i == SW_FROM:
                    strands.begin(sw_strand())
                in_tile(i)
            for half in range(2):
                for n in range(4 * half, 4 * half + 4):
                    def before(j):
                        if j == 1 and n == 3:
                            o_hi(2)
                        elif j == 1 and n in (5, 6):
                            norm_tile(l, 1, n - 5)
                    woven_splits(u_o + 2 * n, 2, before)
                    if n == 7:
                        norm_tile(l, 1, 2)
                    tile_lo(u_o + 2 * n, e_o + 4 * n, (e_o + 4 * n) // 4 * 3, 2)
                if half == 0:
                    strands.finish()
                    o_hi(3)
            norm_tile(l, 1, 3)
            up_pair(0, 0, first=True)
            for part in range(2):
                with act.Fori(1 - part, F_PARTS[part] // 4) as i:
                    up_pair(i, part)
                nu = F_PARTS[part] // 4
                if part == 0:
                    with act.Fori(0, 2) as i:
                        for j in range(2):
                            u = i * (2 * nu) + (u_dn[0] + j * nu)
                            splits(u_dn[0] + j * nu, nu, i, 2 * nu)
                            tile_lo(u, i * 8 + (e_dn[0] + 4 * j), i * 6 + (e_dn[0] // 4 * 3 + 3 * j), nu)
                else:
                    for j in range(4):
                        u = u_dn[1] + j * nu
                        splits(u, 3)
                        if j:
                            norm_tile(l, 2, j - 1)
                        splits(u + 3, nu - 3)
                        tile_lo(u, e_dn[1] + 4 * j, e_dn[1] // 4 * 3 + 3 * j, nu)
                    norm_tile(l, 2, 3)

        with act.Fori(0, DEPTH) as l:
            layer(l)
        rstd(DEPTH, 0)

    @block.vector
    def _(dve):
        V = nc.vector

        def first_lo(j):
            xw = XW0[j].rearrange("p (k t) -> p k t", k=4)
            dve.wait_ge(xhi_ready.sem, xhi_ready.of(0, j + 1))
            V.tensor_tensor(XHL[:, 4 * j:4 * j + 4, T:2 * T], xw, XHL[:, 4 * j:4 * j + 4, 0:T].bitcast(F32),
                            ALU.subtract).then_inc(xlo_ready.sem, 1)

        def first_sums(j):
            dve.wait_ge(sq_ready.sem, sq_ready.of(0, j + 1))
            V.tensor_reduce(PART[:, j, :], SQ0[j].rearrange("p (k t) -> p t k", k=4), AX.X, ALU.add).then_inc(
                part_ready.sem, 1)

        def norm_tile(l, n, j):
            dve.wait_ge(sq_ready.sem, sq_ready.of(l, 4 * n + j + 1))
            V.tensor_reduce(PART[:, j, :], SQ.rearrange("p (k t) -> p t k", k=4), AX.X, ALU.add).then_inc(
                part_ready.sem, 1)
            dve.wait_ge(xhi_ready.sem, xhi_ready.of(l, 4 * n + j + 1))
            V.tensor_tensor(XHL[:, 4 * j:4 * j + 4, T:2 * T], XW.rearrange("p (k t) -> p k t", k=4),
                            XHL[:, 4 * j:4 * j + 4, 0:T].bitcast(F32), ALU.subtract).then_inc(
                                xlo_ready.sem, 1)

        def rstd(l, n):
            dve.wait_ge(colsum_done.sem, colsum_done.of(l, n + 1))
            V.tensor_scalar(MS2, PS[:, 4:6, 0], 1.0 / D, EPS, ALU.mult, ALU.add).then_inc(ms_ready.sem, 1)
            dve.wait_ge(r_ready.sem, r_ready.of(l, n + 1))
            V.tensor_tensor(DIAG.rearrange("p (t c) -> p t c", t=2), IDENT.unsqueeze(1).to_broadcast([P, 2, P]),
                            R2.unsqueeze(2).to_broadcast([P, 2, P]), ALU.mult).then_inc(diag_ready.sem, 1)

        def split(u, s, h):
            dve.wait_ge(whi_ready.sem, u * 2 + (h + 1))
            k = slice(2 * h, 2 * h + 2)
            V.tensor_tensor(w_lo[:, s, k].rearrange("p k n -> p (k n)"),
                            w_raw[:, s, k].rearrange("p k n -> p (k n)"),
                            w_hi[:, s, k].rearrange("p k n -> p (k n)").bitcast(F32), ALU.subtract).then_inc(
                                wlo_ready.sem, 1)

        def split_all(u, s):
            dve.wait_ge(whi_ready.sem, u * 2 + 2)
            V.tensor_tensor(w_lo[:, s].rearrange("p k n -> p (k n)"), w_raw[:, s].rearrange("p k n -> p (k n)"),
                            w_hi[:, s].rearrange("p k n -> p (k n)").bitcast(F32), ALU.subtract).then_inc(
                                wlo_ready.sem, 2)

        dve.sem_inc(sum_ready.sem, 4)
        V.memset(SMALL, -0.5).then_inc(set_up.sem, 1)
        for j in range(AHEAD):
            first_lo(j)
            for h in range(2):
                split(j, j, h)
        first_lo(2)
        first_sums(0)
        first_sums(1)
        first_lo(3)
        first_sums(2)
        first_sums(3)
        dve.wait_ge(io_loaded.sem, 16)
        for r0 in (0, 32):
            V.tensor_tensor(SEL[:, r0 // 4:r0 // 4 + 8], IDENT[:, r0:r0 + 8], IDENT[:, 64 + r0:72 + r0],
                            ALU.add).then_inc(sel_ready.sem, 1)

        def layer(l):

            def splits(u, n, i=0, step=0):
                for j in range(n):
                    v = u + AHEAD + j
                    split_all(l * U_LAYER + (i * step + v), v % SLOTS)

            def woven_splits(u, n, before=None):
                for j in range(n):
                    if before:
                        before(j)
                    v = u + AHEAD + j
                    for h in range(2):
                        split(l * U_LAYER + v, v % SLOTS, h)
                        if j < n - 1:
                            strands.beats(2)

            def add(e, n):
                dve.wait_ge(lo_ready.sem, lo_ready.of(l, e + (n + 1)))
                dve.wait_ge(chunk_done.sem, chunk_done.of(l, e + (n + 1 - 2)))
                V.tensor_tensor(SUM[:, n % 2, :], PS[:, n, 0:T], LO[:, n % 2, :], ALU.add).then_inc(
                    sum_ready.sem, 1)

            def tile_add(e, between=None):
                for n in range(4):
                    add(e, n)
                    strands.beat()
                    if between:
                        between(n)

            def wab_lo():
                dve.wait_ge(wabhi_ready.sem, wabhi_ready.of(l, 1))
                V.tensor_tensor(WABL, WABR, WABH.bitcast(F32), ALU.subtract).then_inc(wablo_ready.sem, 1)

            def in_tile(i):
                def before(j):
                    if i == 0 and j == 2:
                        rstd(l, 0)
                    elif i == 0 and j == 3:
                        wab_lo()
                    elif i == IN_TILES - 1 and j in (1, 2):
                        o_lo(j - 1)
                woven_splits(4 * i, 4, before)
                if i == 0:
                    dve.wait_ge(par_loaded.sem, par_loaded.of(l, 48))
                e, group, c0 = 4 * i, conv_group(IN_ORDER[i]), 4 * n_conv(i)

                def taps(n):
                    for q in range(3):
                        if q == 0:
                            dve.wait_ge(tap0_ready.sem, tap0_ready.of(l, c0 + n + 1))
                        else:
                            dve.wait_ge(tap_done.sem, tap_done.of(l, 3 * (c0 + n) + q))
                        c = PAR_GC + (2 - q) * 24 + group + n
                        V.scalar_tensor_tensor(out=CY[:, n % 2, :], in0=CV[:, n, 2 - q:2 - q + T],
                                               scalar=PAR[:, c:c + 1], in1=CY[:, n % 2, :], op0=ALU.mult,
                                               op1=ALU.add).then_inc(tap_done.sem, 1)
                def conv_strand():
                    for n in range(4):
                        taps(n)
                        yield from beats(2)

                tile_add(e)
                if group is not None:
                    strands.begin(conv_strand())

            def gates_strand():
                W = lambda k: dve.wait_ge(gd.sem, gd.of(l, k))
                yield
                dve.wait_ge(ga.sem, ga.of(l, 1))
                V.tensor_tensor(G[1][0:64, :], PS[0:64, 4, 0:T], G[0][0:64, :], ALU.add).then_inc(gd.sem, 1)
                W(1)
                V.tensor_tensor(G[2][0:64, :], G[1][0:64, :], RSTD[0:64, :], ALU.mult).then_inc(gd.sem, 1)
                W(2)
                V.tensor_scalar(G[5][0:8, :], G[2][0:8, :], GPAR[0:8, 1:2], 0.0, ALU.add, ALU.max).then_inc(
                    gd.sem, 1)
                yield from beats(4)
                dve.wait_ge(ga.sem, ga.of(l, 5))
                V.tensor_tensor(G[5][0:8, :], G[5][0:8, :], G[3][0:8, :], ALU.add).then_inc(gd.sem, 1)
                W(4)
                V.tensor_scalar(G[5][0:8, :], G[5][0:8, :], EXPA[0:8, :], -1.0, ALU.mult, ALU.mult).then_inc(
                    gd.sem, 1)
                V.tensor_scalar(G[4][32:40, :], G[4][32:40, :], 1.0, None, ALU.add).then_inc(gd.sem, 1)
                W(6)
                dve.wait_ge(pads_ready.sem, pads_ready.of(l, 1))
                V.reciprocal(ST[32:40, :], G[4][32:40, :]).then_inc(gd.sem, 1)
                V.tensor_tensor_scan(G[6][0:8, :], con["reset"][0:8, :], G[5][0:8, :], 0.0, ALU.mult,
                                     ALU.add).then_inc(gd.sem, 1)
                W(8)
                g3 = G[6][0:8, :].rearrange("p (n c) -> p n c", c=CH)
                V.tensor_tensor(G[7][0:8, :].rearrange("p (n c) -> p n c", c=CH),
                                g3[:, :, CH - 1:CH].to_broadcast([8, 4, CH]), g3, ALU.subtract).then_inc(
                                    gd.sem, 1)
                V.tensor_scalar(ST[0:8, :], G[6][0:8, :], -1.0, None, ALU.mult).then_inc(gd.sem, 1)
                yield from beats(8)
                dve.wait_ge(gate_t_done.sem, gate_t_done.of(l, 1))
                V.tensor_copy(COL, PS[:, 6, 0:T].rearrange("p (t r) -> p t r", t=2)).then_inc(
                    gate_cols_ready.sem, 1)
                dve.wait_ge(dec_done.sem, dec_done.of(l, 1))
                V.tensor_copy(DEC, PS[:, 7, 0:32]).then_inc(gate_cols_ready.sem, 1)
                dve.wait_ge(sthi_ready.sem, sthi_ready.of(l, 1))
                for r0 in (0, 32):
                    V.tensor_tensor(STR[64 + r0:72 + r0, :], ST[r0:r0 + 8, :], STR[r0:r0 + 8, :].bitcast(F32),
                                    ALU.subtract).then_inc(stlo_ready.sem, 1)
                dve.wait_ge(gate_cols_ready.sem, gate_cols_ready.of(l, 1))
                V.tensor_tensor(BE, COL[:, :, 32:40], COL[:, :, 64:72], ALU.mult).then_inc(
                    gate_cols_ready.sem, 1)

            def gdn_strand():
                yield from beats(GDN_START)
                for g in range(4):
                    yield from gdn(g)

            def gdn(g):
                hh = 2 * g
                for n, a in enumerate((6, 7)):
                    dve.wait_ge(sqn_ready.sem, sqn_ready.of(l, 2 * g + n + 1))
                    V.tensor_reduce(SS[:, 4 * n:4 * n + 4], b4(A[a]), AX.X, ALU.add).then_inc(ss_ready.sem, 1)
                dve.wait_ge(ss_ready.sem, ss_ready.of(l, 3 * g + 2))
                V.tensor_scalar(SS, SS, EPS, None, ALU.add).then_inc(ss_ready.sem, 1)
                yield from beats(GDN_BEATS["keys"] + GDN_BEATS["values"] - 5)
                for n, (a, b, c, need) in enumerate(((0, 4, 1, 1), (3, 4, 0, 1), (1, 4, 2, 2), (4, 5, 3, 3),
                                                     (5, 5, 4, 4))):
                    dve.wait_ge(co_ready.sem, co_ready.of(l, 4 * g + need))
                    f_ = RR[:, 0:4] if c == 0 else CO[:, c - 1, :]
                    V.tensor_tensor(b4(A[a]), b4(PS[:, b, :]), tb(f_), ALU.mult).then_inc(nat_ready.sem, 1)
                    if n == 4:
                        dve.wait_ge(nat_done.sem, nat_done.of(l, 3 * g + 3))
                        V.tensor_tensor(b22(A[2]), b22(PS[:, 6, :]),
                                        COL[:, :, 32 + hh:34 + hh].unsqueeze(3).to_broadcast([P, 2, 2, P]),
                                        ALU.mult).then_inc(nat_ready.sem, 1)
                    yield
                yield from beats(GDN_BEATS["back"])
                dve.wait_ge(grow_done.sem, grow_done.of(l, g + 1))
                for t in range(2):
                    for i in range(2):
                        r = V.scalar_tensor_tensor(out=A[6][:, blk(t, i)], in0=PS[:, 6, blk(t, i)],
                                                   scalar=COL[:, t, hh + i:hh + i + 1], in1=con["gmask"],
                                                   op0=ALU.subtract, op1=ALU.max)
                r.then_inc(gm_ready.sem, 1)
                yield from beats(GDN_BEATS["products"])
                dve.wait_ge(e1_ready.sem, e1_ready.of(l, g + 1))
                dve.wait_ge(qk_done.sem, qk_done.of(l, g + 1))
                V.tensor_tensor(b4(A[9]), PAIR[:, :, 0:P], b4(A[7]), ALU.mult).then_inc(qkg_ready.sem, 1)
                dve.wait_ge(beta_done.sem, beta_done.of(l, g + 1))
                V.tensor_tensor(A[6], PS[:, 6, :], A[7], ALU.mult).then_inc(w1_ready.sem, 1)
                dve.wait_ge(w1_ready.sem, w1_ready.of(l, g + 1))
                V.tensor_tensor(b4(A[3]), PAIR[:, :, P:2 * P], b4(A[6]), ALU.mult).then_inc(at_ready.sem, 1)
                yield from beats(GDN_BEATS["beta"])
                dve.wait_ge(x_done.sem, x_done.of(l, 6 * g + 1))
                V.tensor_tensor(b4(A[4]), IDENT.unsqueeze(1).to_broadcast([P, 4, P]), b4(PS[:, 4, :]),
                                ALU.subtract).then_inc(d_ready.sem, 1)
                yield from beats(GDN_BEATS["transpose"])
                for j in range(1, 6):
                    yield from beats(GDN_BEATS["x"])
                    if j < 5:
                        dve.wait_ge(dx_done.sem, dx_done.of(l, 4 * g + j))
                        V.tensor_tensor(A[4], A[4], PS[:, 4, :], ALU.subtract).then_inc(d_ready.sem, 1)
                    dve.wait_ge(ex_done.sem, ex_done.of(l, 5 * g + j))
                    if j == 1:
                        dve.wait_ge(e0_ready.sem, e0_ready.of(l, g + 1))
                    V.tensor_tensor(A[5], A[5], PS[:, 6, :], ALU.subtract).then_inc(e_ready.sem, 1)
                    yield from beats(GDN_BEATS["e"])
                yield from beats(GDN_BEATS["u"])
                dve.wait_ge(kv_done.sem, kv_done.of(l, g + 1))
                V.tensor_copy(S_[1], PS[:, 4, 0:2 * P]).then_inc(s_ready.sem, 1)
                yield from beats(GDN_BEATS["kv"])
                for n in (1, 2):
                    kvu = PS[:, 5, 0:2 * P] if n == 1 else PS[:, 4, 2 * P:4 * P]
                    dve.wait_ge(s_ready.sem, s_ready.of(l, 3 * g + n))
                    for i in range(2):
                        c = slice(i * P, (i + 1) * P)
                        r = V.scalar_tensor_tensor(out=S_[n + 1][:, c], in0=S_[n][:, c],
                                                   scalar=DEC[:, 4 * (hh + i) + n:4 * (hh + i) + n + 1],
                                                   in1=kvu[:, c], op0=ALU.mult, op1=ALU.add)
                    r.then_inc(ds_ready.sem, 1)
                    dve.wait_ge(mst_done.sem, mst_done.of(l, 2 * g + n))
                    dve.wait_ge(ds_ready.sem, ds_ready.of(l, 2 * g + n))
                    V.tensor_tensor(S_[n + 1], S_[n + 1], PS[:, 6, 0:2 * P], ALU.subtract).then_inc(s_ready.sem, 1)
                    yield from beats(GDN_BEATS["state"])
                dve.wait_ge(ws_done.sem, ws_done.of(l, g + 1))
                v = A[2][CH:P, 0:2 * P]
                V.tensor_tensor(v, v, PS[CH:P, 4, 0:2 * P], ALU.subtract)
                v = A[2][:, 2 * P:4 * P]
                V.tensor_tensor(v, v, PS[:, 4, 2 * P:4 * P], ALU.subtract).then_inc(v_ready.sem, 1)
                yield from beats(GDN_BEATS["ws"] + GDN_BEATS["out"])
                dve.wait_ge(osum_done.sem, osum_done.of(l, g + 1))
                V.tensor_scalar(MSO, PS[:, 6, 0:4], 1.0 / P, EPS, ALU.mult, ALU.add).then_inc(mso_ready.sem, 1)
                dve.wait_ge(ro_ready.sem, ro_ready.of(l, g + 1))
                V.tensor_tensor(b4(A[4]), IDENT.unsqueeze(1).to_broadcast([P, 4, P]), tb(RO),
                                ALU.mult).then_inc(odiag_ready.sem, 1)
                yield from beats(GDN_BEATS["sums"])
                dve.wait_ge(orow_done.sem, orow_done.of(l, g + 1))
                dve.wait_ge(oz_ready.sem, oz_ready.of(l, g + 1))
                V.tensor_tensor(pair(QKV, hh), b22(A[5]), b22(PS[:, 4, :]), ALU.mult).then_inc(gdn_out.sem, 1)
                yield from beats(GDN_BEATS["rows"])

            def sb_strand():
                yield from beats(4)
                for h in range(SH):
                    dve.wait_ge(sb_ln.sem, sb_ln.of(l, h + 1))
                    V.scalar_tensor_tensor(out=SBL, in0=SBZ, scalar=0.0, in1=SBL,
                                           op0=ALU.max, op1=ALU.add).then_inc(sb_sp.sem, 1)
                    dve.wait_ge(sb_sp.sem, sb_sp.of(l, 2 * h + 1))
                    V.tensor_tensor(SBL, SBL, con["sbmask"], ALU.mult).then_inc(sb_sp.sem, 1)
                    yield from beats(SB_BEATS[0])
                    dve.wait_ge(sb_c_done.sem, sb_c_done.of(l, h + 1))
                    dve.wait_ge(sb_zm.sem, sb_zm.of(l, h + 1))
                    V.tensor_tensor(SBM, SBM, PS[:, 7, 0:384], ALU.add).then_inc(sb_y.sem, 1)
                    yield from beats(SB_BEATS[1] + SB_BEATS[2])

            def sw_strand():
                yield from beats(8)
                for c in range(3):
                    x = SWX[:, 2 * c:2 * c + 2, :]
                    dve.wait_ge(rot_done.sem, rot_done.of(l, c + 1))
                    if c:
                        dve.wait_ge(roped.sem, roped.of(l, c))
                    V.tensor_tensor(SWP.rearrange("p (a t) -> p a t", a=2),
                                    PS[:, 7, :].rearrange("p (a t) -> p a t", a=2),
                                    con["sin"].unsqueeze(1).to_broadcast([P, 2, T]), ALU.mult).then_inc(xsin.sem, 1)
                    dve.wait_ge(xsin.sem, xsin.of(l, c + 1))
                    dve.wait_ge(xcos.sem, xcos.of(l, c + 1))
                    V.tensor_tensor(x, SWS.rearrange("p (a t) -> p a t", a=2),
                                    SWP.rearrange("p (a t) -> p a t", a=2), ALU.add).then_inc(roped.sem, 1)
                    yield from beats((3, 6, 1)[c])
                yield
                for h in range(WH_):
                    dve.wait_ge(sw_s_done.sem, sw_s_done.of(l, h + 1))
                    if h:
                        dve.wait_ge(sw_den.sem, sw_den.of(l, 3 * h))
                    V.scalar_tensor_tensor(out=SWS, in0=PS[:, 7, :], scalar=SCALE, in1=con["swaadd"],
                                           op0=ALU.mult, op1=ALU.add).then_inc(sw_s.sem, 1)
                    dve.wait_ge(sw_s.sem, sw_s.of(l, 3 * h + 1))
                    V.tensor_reduce(MX, SWS.rearrange("p (t k) -> p t k", t=2), AX.X, ALU.max).then_inc(sw_s.sem, 1)
                    dve.wait_ge(sw_s.sem, sw_s.of(l, 3 * h + 2))
                    V.tensor_scalar(NM, MX, PAR[:, PAR_SK + h:PAR_SK + h + 1], -1.0, ALU.max, ALU.mult).then_inc(
                        sw_s.sem, 1)
                    yield
                    dve.wait_ge(sw_p.sem, sw_p.of(l, 3 * h + 3))
                    V.tensor_tensor(DEN, SUMP, SE, ALU.add).then_inc(sw_den.sem, 1)
                    dve.wait_ge(sw_den.sem, sw_den.of(l, 3 * h + 1))
                    V.reciprocal(REC, DEN).then_inc(sw_den.sem, 1)
                    dve.wait_ge(sw_den.sem, sw_den.of(l, 3 * h + 2))
                    p3 = SWP.rearrange("p (t k) -> p t k", t=2)
                    V.tensor_tensor(p3, p3, REC.unsqueeze(2).to_broadcast([P, 2, T]), ALU.mult).then_inc(
                        sw_den.sem, 1)
                    yield from beats(sum(SW_BEATS) - 1)

            def o_lo(kg):
                src = (QKV[:, 0:4, :], SBX[:, 0:4, :], QKV[:, 4:8, :], SWX[:, 0:4, :])[kg]
                dve.wait_ge(ohi_ready.sem, ohi_ready.of(l, kg + 1))
                V.tensor_tensor(XHL[:, 4 * kg:4 * kg + 4, T:2 * T], src,
                                XHL[:, 4 * kg:4 * kg + 4, 0:T].bitcast(F32), ALU.subtract).then_inc(
                                    olo_ready.sem, 1)

            def up_pair(i, part, first=False):
                u, e = i * 8 + u_up[part], i * 8 + e_up[part]
                f0 = sum(F_PARTS[:part])
                fc = i * 4 + f0
                if first:
                    splits(u_up[part], 2)
                    rstd(l, 1)
                    splits(u_up[part] + 2, 2)
                else:
                    splits(u_up[part], 4, i, 8)

                def taps(n):
                    for q in range(2):
                        if q == 0:
                            dve.wait_ge(gtap0_ready.sem, gtap0_ready.of(l, fc + (n + 1)))
                        else:
                            dve.wait_ge(gtap_done.sem, gtap_done.of(l, fc * 2 + (2 * n + 1)))
                        V.scalar_tensor_tensor(out=GY[:, n, :], in0=GP[:, n, 1 - q:1 - q + T],
                                               scalar=PAR[:, bass.ds(fc + (PAR_FCW + (1 - q) * FC + n), 1)],
                                               in1=GY[:, n, :], op0=ALU.mult, op1=ALU.add).then_inc(
                                                   gtap_done.sem, 1)
                tile_add(e, lambda n: taps(n - 2) if n >= 2 else None)
                splits(u_up[part] + 4, 1, i, 8)
                taps(2)
                taps(3)
                splits(u_up[part] + 5, 3, i, 8)

                def low(n):
                    dve.wait_ge(midhi_ready.sem, midhi_ready.of(l, fc + (n + 1)))
                    V.tensor_tensor(MID[:, bass.ds(i * 4 + n, 1), T:2 * T], VV[:, n:n + 1, :],
                                    MID[:, bass.ds(i * 4 + n, 1), 0:T].bitcast(F32), ALU.subtract).then_inc(
                                        midlo_ready.sem, 1)
                tile_add(e + 4, lambda n: low(0) if n == 3 else None)
                for n in (1, 2, 3):
                    low(n)

            strands = Strands()
            for i in range(IN_TILES):
                if i == GATES_FROM:
                    strands.begin(gates_strand())
                if i == GDN_FROM:
                    strands.begin(gdn_strand())
                if i == SB_FROM:
                    strands.begin(sb_strand())
                if i == SW_FROM:
                    strands.begin(sw_strand())
                in_tile(i)
            for half in range(2):
                for n in range(4 * half, 4 * half + 4):
                    def before(j):
                        if j == 1 and n == 3:
                            o_lo(2)
                        elif j == 1 and n in (5, 6):
                            norm_tile(l, 1, n - 5)
                    woven_splits(u_o + 2 * n, 2, before)
                    if n == 7:
                        norm_tile(l, 1, 2)
                    tile_add(e_o + 4 * n)
                if half == 0:
                    strands.finish()
                    o_lo(3)
            norm_tile(l, 1, 3)
            up_pair(0, 0, first=True)
            for part in range(2):
                with dve.Fori(1 - part, F_PARTS[part] // 4) as i:
                    up_pair(i, part)
                nu = F_PARTS[part] // 4
                if part == 0:
                    with dve.Fori(0, 2) as i:
                        for j in range(2):
                            splits(u_dn[0] + j * nu, nu, i, 2 * nu)
                            tile_add(i * 8 + (e_dn[0] + 4 * j))
                else:
                    for j in range(4):
                        splits(u_dn[1] + j * nu, 3)
                        if j:
                            norm_tile(l, 2, j - 1)
                        splits(u_dn[1] + j * nu + 3, nu - 3)
                        tile_add(e_dn[1] + 4 * j)
                    norm_tile(l, 2, 3)

        with dve.Fori(0, DEPTH) as l:
            layer(l)
        rstd(DEPTH, 0)
        for j in (2, 3):
            x4 = XT[:, 4 * j:4 * j + 4, :]
            k = NORMS * KC - KC + 4 * j
            V.tensor_tensor(x4, x4, NW[:, k:k + 4].unsqueeze(2).to_broadcast([P, 4, T]), ALU.mult).then_inc(
                last_xw.sem, 1)
        dve.wait_ge(rstd_ready.sem, rstd_ready.of(DEPTH, 1))
        dve.wait_ge(fin_xw.sem, 2)
        dve.wait_ge(last_xw.sem, 2)
        for j in range(4):
            x4 = XT[:, 4 * j:4 * j + 4, :]
            V.tensor_tensor(x4, x4, RSTD.unsqueeze(1).to_broadcast([P, 4, T]), ALU.mult).then_inc(fin_y.sem, 1)

    @block.gpsimd
    def _(pool):
        Q = nc.gpsimd

        pool.sem_inc(chunk_done.sem, 2)
        pool.wait_ge(nw_loaded.sem, 16)
        for j in range(4):
            pool.wait_ge(x_loaded[j].sem, 16)
            nc.gpsimd.tensor_tensor(XW0[j].rearrange("p (k t) -> p k t", k=4), XT[:, 4 * j:4 * j + 4, :],
                                    NW[:, 4 * j:4 * j + 4].unsqueeze(2).to_broadcast([P, 4, T]),
                                    ALU.mult).then_inc(xw_ready.sem, 1)
        pool.wait_ge(io_loaded.sem, 16)

        def power(dst, src, n, done):
            Q.tensor_tensor(dst, src, MHALF[:, 0:n], ALU.pow).then_inc(done, 1)

        def layer(l):

            def finish(e, n, dst):
                pool.wait_ge(sum_ready.sem, sum_ready.of(l, e + (n + 1)))
                Q.tensor_tensor(dst, SUM[:, n % 2, :], RSTD, ALU.mult).then_inc(chunk_done.sem, 1)

            def residual(e, n, x):
                pool.wait_ge(sum_ready.sem, sum_ready.of(l, e + (n + 1)))
                Q.tensor_tensor(x, x, SUM[:, n % 2:n % 2 + 1, :], ALU.add).then_inc(chunk_done.sem, 1)

            def norm_xw(n, j):
                done = (E_IN + 16 if n == 1 else E_LAYER - 16) + 4 * j + 4
                pool.wait_ge(chunk_done.sem, chunk_done.of(l, done))
                pool.wait_ge(xlo_ready.sem, xlo_ready.of(l, 4 * n + j))
                w = NW[:, bass.ds(l * (2 * KC) + (n * KC + 4 * j), 4)]
                Q.tensor_tensor(XW.rearrange("p (k t) -> p k t", k=4), XT[:, 4 * j:4 * j + 4, :],
                                w.unsqueeze(2).to_broadcast([P, 4, T]), ALU.mult).then_inc(xw_ready.sem, 1)

            Q.dma_start(PAR[:, 0:PAR_N], params[bass.ds(l, 1)].rearrange("a p n -> p (a n)")).then_inc(
                par_loaded.sem, 16)
            Q.dma_start(GPAR[0:8, 0:2], gate_par[bass.ds(l, 1)].rearrange("a p n -> p (a n)")).then_inc(
                par_loaded.sem, 16)
            Q.dma_start(WABR, wab[bass.ds(l, 1)].rearrange("a p n -> p (a n)")).then_inc(wab_loaded.sem, 16)
            Q.dma_start(CON, consts).then_inc(par_loaded.sem, 16)
            Q.memset(ST, 0.0).then_inc(pads_ready.sem, 1)
            Q.memset(CV[:, :, 0:3], 0.0)
            pool.wait_ge(ms_ready.sem, ms_ready.of(l, 1))
            power(R2, MS2, 2, r_ready.sem)

            def gdn_strand():
                yield from beats(GDN_START)
                for g in range(4):
                    yield from gdn(g)

            def gdn(g):
                hh = 2 * g
                rk, rq = RR[:, 0:4], RR[:, 4:8]
                r3 = lambda a: a.rearrange("p (t i) -> p t i", t=2)
                pool.wait_ge(ss_ready.sem, ss_ready.of(l, 3 * g + 3))
                if g:
                    pool.wait_ge(gdn_out.sem, gdn_out.of(l, g))
                power(RR, SS, 8, rr_ready.sem)
                pool.wait_ge(rr_ready.sem, rr_ready.of(l, g + 1))
                if g == 0:
                    pool.wait_ge(gate_cols_ready.sem, gate_cols_ready.of(l, 3))
                Q.tensor_tensor(r3(CO[:, 0, :]), r3(rk), BE[:, :, hh:hh + 2], ALU.mult).then_inc(co_ready.sem, 1)
                Q.tensor_tensor(r3(CO[:, 1, :]), r3(rk), COL[:, :, 96 + hh:98 + hh], ALU.mult).then_inc(
                    co_ready.sem, 1)
                Q.tensor_scalar(CO[:, 2, :], rq, SCALE, None, ALU.mult).then_inc(co_ready.sem, 1)
                pool.wait_ge(co_ready.sem, co_ready.of(l, 4 * g + 3))
                Q.tensor_tensor(r3(CO[:, 3, :]), r3(CO[:, 2, :]), COL[:, :, 64 + hh:66 + hh], ALU.mult).then_inc(
                    co_ready.sem, 1)
                yield from beats(GDN_BEATS["keys"] + GDN_BEATS["values"] + GDN_BEATS["back"] + GDN_BEATS["products"])
                pool.wait_ge(at_ready.sem, at_ready.of(l, g + 1))
                for j in range(6):
                    bt = A[8] if j % 2 == 0 else A[6]
                    if j >= 2:
                        pool.wait_ge(x_done.sem, x_done.of(l, 6 * g + j - 1))
                        pool.wait_ge(e0_ready.sem, e0_ready.of(l, g + 1))
                    Q.tensor_tensor(b4(bt), b4(A[3]),
                                    con["level"][:, j * P:(j + 1) * P].unsqueeze(1).to_broadcast([P, 4, P]),
                                    ALU.mult).then_inc(bt_ready.sem, 1)
                    if j == 0:
                        pool.wait_ge(bt_ready.sem, bt_ready.of(l, 6 * g + 1))
                        Q.tensor_tensor(b4(A[5]), IDENT.unsqueeze(1).to_broadcast([P, 4, P]), b4(A[8]),
                                        ALU.subtract).then_inc(e0_ready.sem, 1)
                    else:
                        yield from beats(GDN_BEATS["beta"] + GDN_BEATS["transpose"] if j == 1 else GDN_BEATS["x"] + GDN_BEATS["e"])
                yield from beats(GDN_BEATS["x"] + GDN_BEATS["e"])
                yield from beats(GDN_BEATS["u"] + GDN_BEATS["kv"] + 2 * GDN_BEATS["state"] + GDN_BEATS["ws"])
                pool.wait_ge(os_ready.sem, os_ready.of(l, g + 1))
                pool.wait_ge(silu_done.sem, silu_done.of(l, 4 * n_silu(4 if g < 2 else 11)))
                Q.tensor_tensor(b22(A[5]), b22(A[5]), pair(Z, hh), ALU.mult).then_inc(oz_ready.sem, 1)
                yield from beats(GDN_BEATS["out"])
                pool.wait_ge(mso_ready.sem, mso_ready.of(l, g + 1))
                power(RO, MSO, 4, ro_ready.sem)
                yield from beats(GDN_BEATS["sums"] + GDN_BEATS["rows"])

            def sb_strand():
                yield from beats(4)
                for h in range(SH):
                    pool.wait_ge(sb_zs.sem, sb_zs.of(l, h + 1))
                    if h:
                        pool.wait_ge(sb_a.sem, sb_a.of(l, h))
                    Q.tensor_tensor(SBM, SBZ, con["sbadd"], ALU.add).then_inc(sb_zm.sem, 1)
                    yield from beats(sum(SB_BEATS))

            def sw_strand():
                yield from beats(4)
                for c in range(3):
                    if c:
                        pool.wait_ge(roped.sem, roped.of(l, c))
                    else:
                        pool.wait_ge(sb_out.sem, sb_out.of(l, 4))
                    pool.wait_ge(chunk_done.sem, chunk_done.of(l, 48 if c < 2 else 52))
                    Q.tensor_tensor(SWS.rearrange("p (a t) -> p a t", a=2), SWX[:, 2 * c:2 * c + 2, :],
                                    con["cos"].unsqueeze(1).to_broadcast([P, 2, T]), ALU.mult).then_inc(xcos.sem, 1)
                    yield from beats((6, 7, 1)[c])

            strands = Strands()
            for i in range(IN_TILES):
                if i == GDN_FROM:
                    strands.begin(gdn_strand())
                if i == SB_FROM:
                    strands.begin(sb_strand())
                if i == SW_FROM:
                    strands.begin(sw_strand())
                strands.beats(12)
                name, e = IN_ORDER[i], 4 * i
                for n in range(4):
                    if conv_group(name) is not None:
                        if i:
                            pool.wait_ge(tap_done.sem, tap_done.of(l, 3 * (4 * n_conv(i) - 4 + n) + 3))
                        dst = CV[:, n, 3:3 + T]
                    elif name[0] == "z":
                        dst = Z[:, 4 * int(name[1]) + n, :]
                    elif name[:2] == "sb":
                        dst = SBX[:, 4 * int(name[2]) + n, :]
                    else:
                        dst = SWX[:, 4 * int(name[2]) + n, :]
                        pool.wait_ge(silu_done.sem, silu_done.of(l, 4 * n_silu(IN_TILES)))
                    finish(e, n, dst)
                    strands.beat()
            for half in range(2):
                for n8 in range(4 * half, 4 * half + 4):
                    strands.beats(4)
                    for n in range(4):
                        c = 4 * (n8 % 4) + n
                        residual(e_o + 4 * n8, n, XT[:, c:c + 1, :])
                        strands.beat()
                    if half == 1:
                        norm_xw(1, n8 - 4)
                strands.finish()
            pool.wait_ge(olo_ready.sem, olo_ready.of(l, 4))
            zeros = IDENT[:, 0:8].rearrange("p (s c) -> p s c", s=4)
            Q.tensor_tensor(GP[:, :, 0:2], zeros, zeros, ALU.subtract)
            pool.wait_ge(ms_ready.sem, ms_ready.of(l, 2))
            power(R2, MS2, 2, r_ready.sem)
            for part in range(2):
                with pool.Fori(0, F_PARTS[part] // 4) as i:
                    e = i * 8 + e_up[part]
                    fc = i * 4 + sum(F_PARTS[:part])
                    pool.wait_ge(rstd_ready.sem, rstd_ready.of(l, 2))
                    for n in range(4):
                        finish(e, n, GP[:, n, 2:2 + T])
                    for n in range(4):
                        pool.wait_ge(sum_ready.sem, sum_ready.of(l, e + (4 + n + 1)))
                        Q.tensor_tensor(VV[:, n, :], SUM[:, n % 2, :], RSTD, ALU.mult).then_inc(
                            chunk_done.sem, 1)
                        pool.wait_ge(chunk_done.sem, chunk_done.of(l, e + (4 + n + 1)))
                        pool.wait_ge(gsilu_done.sem, gsilu_done.of(l, fc + (n + 1)))
                        Q.tensor_tensor(VV[:, n, :], VV[:, n, :], GY[:, n, :], ALU.mult).then_inc(
                            gated_done.sem, 1)
                if part == 0:
                    with pool.Fori(0, 2) as i:
                        for j in range(2):
                            for n in range(4):
                                residual(i * 8 + (e_dn[0] + 4 * j), n, XT[:, bass.ds(i * 8 + (4 * j + n), 1), :])
                else:
                    for j in range(4):
                        for n in range(4):
                            residual(e_dn[1] + 4 * j, n, XT[:, 4 * j + n:4 * j + n + 1, :])
                        norm_xw(2, j)

        with pool.Fori(0, DEPTH) as l:
            layer(l)
        for j in range(2):
            pool.wait_ge(sq_ready.sem, sq_ready.of(DEPTH, j + 1))
            pool.wait_ge(xw_ready.sem, xw_ready.of(DEPTH, j + 1))
            x4 = XT[:, 4 * j:4 * j + 4, :]
            k = NORMS * KC - KC + 4 * j
            Q.tensor_tensor(x4, x4, NW[:, k:k + 4].unsqueeze(2).to_broadcast([P, 4, T]), ALU.mult).then_inc(
                fin_xw.sem, 1)
        pool.wait_ge(ms_ready.sem, ms_ready.of(DEPTH, 1))
        power(R2, MS2, 2, r_ready.sem)

    block.__exit__(None, None, None)


def _unit(w):
    return w.reshape(4, 128, 512).transpose(1, 0, 2).reshape(128, 2048)


def _shape_constants():
    import numpy as np
    c = {}
    i = np.arange(128)
    rot = np.zeros((128, 128), np.float32)
    rot[i[64:], i[:64]] = -1.0
    rot[i[:64], i[64:]] = 1.0
    c["rot"] = rot
    c["negu"] = -(i[:, None] >= i[None, :]).astype(np.float32)
    c["negone"] = -np.ones((128, 128), np.float32)
    up = (i[None, :] > i[:, None]).astype(np.float32)
    c["sbmask"] = np.concatenate([up, np.ones((128, 128), np.float32), up], 1)
    c["sbadd"] = np.where(c["sbmask"] > 0, 0.0, -1e30).astype(np.float32)
    half = 64
    inv = np.float32(10000.0) ** (-np.arange(half, dtype=np.float32) / np.float32(half))
    ang = (np.arange(256, dtype=np.float32)[:, None] * inv[None, :].astype(np.float32)).astype(np.float32)
    c["cos"] = np.tile(np.cos(ang).T, (2, 1)).astype(np.float32)
    c["sin"] = np.tile(np.sin(ang).T, (2, 1)).astype(np.float32)
    q = np.arange(128)
    k = np.arange(256)
    m = []
    for t in range(2):
        nq, nk = (2 * t + q // 64)[:, None], (k // 64)[None, :]
        m.append(np.where((nk == nq) | (nk == nq - 1), 0.0, -1e30))
    c["swaadd"] = np.concatenate(m, 1).astype(np.float32)
    same = (i[:, None] // 64 == i[None, :] // 64)
    c["gmask"] = np.where(same & (i[None, :] >= i[:, None]), 0.0, 1e30).astype(np.float32)
    lev = []
    for j in range(6):
        b = 2 ** j
        lev.append(((i[:, None] // (2 * b) == i[None, :] // (2 * b)) & (i[:, None] // b % 2 == 0)
                    & (i[None, :] // b % 2 == 1)).astype(np.float32))
    c["level"] = np.concatenate(lev, 1)
    c["reset"] = np.tile((np.arange(256) % 64 != 0).astype(np.float32), (128, 1))
    return np.ascontiguousarray(np.concatenate([c[n] for n in CONST], 1))


def _layout(a):
    import numpy as np
    units = np.zeros((U_ALL + SLOTS, 128, 2048), np.float32)
    wab = np.zeros((DEPTH, 128, 17, 64), np.float32)
    par = np.zeros((DEPTH, 128, PAR_N), np.float32)
    cols = {"q0": 1536, "k0": 2560, "v0": 3584, "q1": 2048, "k1": 3072, "v1": 4096, "z0": 4608, "z1": 5120,
            "sb0": 0, "sb1": 512, "sb2": 1024, "sw0": 5648, "sw1": 6160}
    in_cols = [cols[n] for n in IN_ORDER]
    for l in range(DEPTH):
        u = l * U_LAYER
        for c in in_cols:
            for k in range(4):
                units[u] = _unit(a["w_in"][l, k * 512:(k + 1) * 512, c:c + 512])
                u += 1
        k_rows = [512, 0, 1024, 1536]
        for half in range(2):
            for n in range(4):
                for k in k_rows[2 * half:2 * half + 2]:
                    units[u] = _unit(a["w_o"][l, k:k + 512, n * 512:(n + 1) * 512])
                    u += 1
        f0 = 0
        for part in F_PARTS:
            for i in range(part // 4):
                for base in (0, DFF):
                    c = base + (f0 + 4 * i) * 128
                    for k in range(4):
                        units[u] = _unit(a["w_up"][l, k * 512:(k + 1) * 512, c:c + 512])
                        u += 1
            for n in range(4):
                for k in range(part // 4):
                    r = (f0 + 4 * k) * 128
                    units[u] = _unit(a["w_down"][l, r:r + 512, n * 512:(n + 1) * 512])
                    u += 1
            f0 += part
        ab = a["w_in"][l, :, 5632:5648].reshape(16, 128, 16).transpose(1, 0, 2)
        wab[l, :, 0:16, 0:8] = ab[:, :, 0:8]
        wab[l, :, 0:16, 32:40] = ab[:, :, 8:16]
        par[l, :, PAR_GC:PAR_GC + 96] = a["gdn_conv"][l].reshape(96, 128).T
        par[l, :, PAR_FCW:PAR_FCW + 132] = a["ffn_conv"][l].reshape(132, 128).T
        par[l, :, PAR_FB:PAR_FB + 44] = a["ffn_conv_bias"][l].reshape(44, 128).T
        par[l, :, PAR_GN] = a["gdn_norm"][l]
        par[l, :, PAR_SK:PAR_SK + 4] = a["swa_sinks"][l][None, :]
    gate = np.stack([a["gdn_a_log"], a["gdn_dt_bias"]], 2)
    x = np.ascontiguousarray(a["x"][0].T.reshape(16, 128, 256).transpose(1, 0, 2))
    io = np.concatenate([np.eye(128, dtype=np.float32), np.ones((128, 128), np.float32)], 1)
    norms = [a[n][l] for l in range(DEPTH) for n in ("attn_norm", "ffn_norm")] + [a["final_norm"]]
    nw = np.ascontiguousarray(np.concatenate([w.reshape(16, 128).T for w in norms], 1))
    return {"units": units, "wab": wab.reshape(DEPTH, 128, 17 * 64), "params": par, "gate_par": np.ascontiguousarray(gate),
            "consts": _shape_constants(), "ident_ones": io, "x_in": x, "norm_w": nw}


def kernel(**inputs):
    import numpy as np
    import concourse.bacc as bacc
    from concourse.bass_utils import run_bass_kernel_spmd

    arrays = _layout({k: np.asarray(v) for k, v in inputs.items()})
    nc = bacc.Bacc("TRN2", target_bir_lowering=False, num_devices=1)
    aps = {n: nc.dram_tensor(n, a.shape, F32, kind="ExternalInput").ap() for n, a in arrays.items()}
    out = nc.dram_tensor("out", (128, 16, 256), F32, kind="ExternalOutput").ap()
    build(nc, **aps, out=out)
    r = run_bass_kernel_spmd(nc, [arrays], core_ids=[0])
    y = r.results[0]["out"]
    return y.transpose(1, 0, 2).reshape(2048, 256).T.reshape(1, 256, 2048)
```
